# Optimizing a Trainium2 kernel written in Bass

```python
import jax, jax.numpy as jnp
from jax import lax
import numpy as np

D_MODEL = 1024
BATCH = 1
SEQ = 512
DEPTH = 1

D_MIX = D_MODEL
D_A = D_MIX // 2
D_B = D_MIX - D_A
HEAD_DIM = 64
N_GROUPS_A = D_A // HEAD_DIM
N_GROUPS_B = D_B // HEAD_DIM
K_SHORT = 3
K_CONFORMER = 31
K_FFN = 3
D_FF = 2816
D_IN = 3 * D_A + 2 * D_B
RMS_EPS = 1e-6
LN_EPS = 1e-5


def rmsnorm(x, g):
    xf = x.astype(jnp.float32)
    y = xf * lax.rsqrt(jnp.mean(xf * xf, axis=-1, keepdims=True) + RMS_EPS)
    return (y * g.astype(jnp.float32)).astype(x.dtype)

def layernorm(x, g, b):
    xf = x.astype(jnp.float32)
    mu = jnp.mean(xf, axis=-1, keepdims=True)
    var = jnp.mean(jnp.square(xf - mu), axis=-1, keepdims=True)
    y = (xf - mu) * lax.rsqrt(var + LN_EPS)
    return (y * g.astype(jnp.float32) + b.astype(jnp.float32)).astype(x.dtype)

def dwconv(x, w):
    k, c = w.shape
    rhs = w[:, None, :].astype(x.dtype)
    return lax.conv_general_dilated(
        x, rhs, window_strides=(1,), padding=[(k // 2, k // 2)],
        dimension_numbers=("NWC", "WIO", "NWC"), feature_group_count=c)

def first_inputs(seed: int = 0) -> dict:
    key = jax.random.key(seed)
    ks = jax.random.split(key, 16)
    f32 = jnp.float32

    def nrm(k, shape, scale):
        return jax.random.normal(k, shape, f32) * scale

    return {
        "x": jax.random.normal(ks[0], (BATCH, SEQ, D_MODEL), f32),
        "norm_mix_g": 1.0 + nrm(ks[1], (DEPTH, D_MODEL), 0.05),
        "w_in": nrm(ks[2], (DEPTH, D_MODEL, D_IN), D_MODEL ** -0.5),
        "conv_a_w": nrm(ks[3], (DEPTH, K_SHORT, D_A), K_SHORT ** -0.5),
        "conv_b_w": nrm(ks[4], (DEPTH, K_CONFORMER, D_B), K_CONFORMER ** -0.5),
        "conv_b_b": nrm(ks[5], (DEPTH, D_B), 0.02),
        "ln_b_g": 1.0 + nrm(ks[6], (DEPTH, D_B), 0.05),
        "ln_b_b": nrm(ks[7], (DEPTH, D_B), 0.02),
        "w_out": nrm(ks[8], (DEPTH, D_MIX, D_MODEL), D_MIX ** -0.5),
        "norm_ffn_g": 1.0 + nrm(ks[9], (DEPTH, D_MODEL), 0.05),
        "w_gate": nrm(ks[10], (DEPTH, D_MODEL, D_FF), D_MODEL ** -0.5),
        "w_up": nrm(ks[11], (DEPTH, D_MODEL, D_FF), D_MODEL ** -0.5),
        "conv_ffn_w": nrm(ks[12], (DEPTH, K_FFN, D_FF), K_FFN ** -0.5),
        "w_down": nrm(ks[13], (DEPTH, D_FF, D_MODEL), D_FF ** -0.5),
        "norm_final_g": 1.0 + nrm(ks[14], (D_MODEL,), 0.05),
    }

def first_block(x, norm_mix_g, w_in, conv_a_w, conv_b_w, conv_b_b, ln_b_g, ln_b_b,
              w_out, norm_ffn_g, w_gate, w_up, conv_ffn_w, w_down, norm_final_g):
    for l in range(DEPTH):
        h = rmsnorm(x, norm_mix_g[l])
        z = jnp.einsum("bsd,de->bse", h, w_in[l])
        a_h, a_bg, a_cg, b_val, b_gate = jnp.split(
            z, [D_A, 2 * D_A, 3 * D_A, 3 * D_A + D_B], axis=-1)
        y_a = a_bg * dwconv(a_cg * a_h, conv_a_w[l])
        u = b_val * jax.nn.sigmoid(b_gate)
        u = dwconv(u, conv_b_w[l]) + conv_b_b[l].astype(u.dtype)
        y_b = jax.nn.silu(layernorm(u, ln_b_g[l], ln_b_b[l]))
        y = jnp.concatenate([y_a, y_b], axis=-1)
        x = x + jnp.einsum("bse,ed->bsd", y, w_out[l])

        h = rmsnorm(x, norm_ffn_g[l])
        g = dwconv(jnp.einsum("bsd,df->bsf", h, w_gate[l]), conv_ffn_w[l])
        v = jnp.einsum("bsd,df->bsf", h, w_up[l])
        x = x + jnp.einsum("bsf,fd->bsd", jax.nn.silu(g) * v, w_down[l])

    return rmsnorm(x, norm_final_g)


DEPTH_2 = 2

CHUNK = 64
N_MIXERS = 2
RET_HEADS = 4
RET_DK = D_MODEL // RET_HEADS
RET_DV = 2 * RET_DK
RET_QK = RET_HEADS * RET_DK
RET_VW = RET_HEADS * RET_DV
ROPE_BASE = 10000.0
ATT_HEADS = 16
ATT_DH = D_MODEL // ATT_HEADS
PAST_CHUNKS = 8
BAND_PAST = PAST_CHUNKS * CHUNK
BAND = (PAST_CHUNKS + 1) * CHUNK
MAX_REL = 256
REL_TABLE = MAX_REL + CHUNK
D_FF_2 = 4 * D_MODEL
EPS = 1e-6


def _rmsnorm(x, g):
    xf = x.astype(jnp.float32)
    y = xf * lax.rsqrt(jnp.mean(xf * xf, axis=-1, keepdims=True) + EPS)
    return (y * g.astype(jnp.float32)).astype(x.dtype)

def _rope(t, pos):
    d = t.shape[-1]
    half = d // 2
    inv = jnp.exp(-jnp.log(ROPE_BASE) * jnp.arange(half, dtype=jnp.float32) / half)
    ang = pos[:, None] * inv[None, :]
    cos = jnp.cos(ang)[None, :, None, :]
    sin = jnp.sin(ang)[None, :, None, :]
    tf = t.astype(jnp.float32)
    t1, t2 = tf[..., :half], tf[..., half:]
    return jnp.concatenate([t1 * cos - t2 * sin, t1 * sin + t2 * cos], axis=-1).astype(t.dtype)

def _retention(h, w_in, gn_g, w_out):
    B, S, _ = h.shape
    nc = S // CHUNK
    proj = h @ w_in
    q, k, v, g = jnp.split(proj, [RET_QK, 2 * RET_QK, 2 * RET_QK + RET_VW], axis=-1)
    q = q.reshape(B, S, RET_HEADS, RET_DK)
    k = k.reshape(B, S, RET_HEADS, RET_DK)
    v = v.reshape(B, S, RET_HEADS, RET_DV)
    pos = jnp.arange(S, dtype=jnp.float32)
    q = _rope(q, pos)
    k = _rope(k, pos) * (RET_DK ** -0.5)

    def to_chunks(t):
        return t.reshape(B, nc, CHUNK, RET_HEADS, t.shape[-1]).transpose(1, 0, 3, 2, 4)

    qc, kc, vc = to_chunks(q), to_chunks(k), to_chunks(v)
    dt = q.dtype
    log_gamma = jnp.log1p(-jnp.exp2(-5.0 - jnp.arange(RET_HEADS, dtype=jnp.float32)))
    idx = jnp.arange(CHUNK, dtype=jnp.float32)
    intra_decay = jnp.exp(log_gamma[:, None, None] * jnp.abs(idx[:, None] - idx[None, :])).astype(dt)
    key_decay = jnp.exp(log_gamma[:, None] * (CHUNK - 1 - idx)[None, :]).astype(dt)
    query_decay = jnp.exp(log_gamma[:, None] * (idx + 1.0)[None, :]).astype(dt)
    chunk_decay = jnp.exp(log_gamma * CHUNK).astype(dt)

    def step(state, inp):
        qb, kb, vb = inp
        scores = jnp.einsum('bhid,bhjd->bhij', qb, kb) * intra_decay[None]
        o_intra = jnp.einsum('bhij,bhje->bhie', scores, vb)
        o_cross = jnp.einsum('bhid,bhde->bhie', qb, state) * query_decay[None, :, :, None]
        new_state = (state * chunk_decay[None, :, None, None]
                     + jnp.einsum('bhjd,bhje->bhde', kb * key_decay[None, :, :, None], vb))
        return new_state, o_intra + o_cross

    state0 = jnp.zeros((B, RET_HEADS, RET_DK, RET_DV), dt)
    _, o = lax.scan(step, state0, (qc, kc, vc))
    o = o.transpose(1, 0, 3, 2, 4).reshape(B, S, RET_HEADS, RET_DV).astype(jnp.float32)
    mu = jnp.mean(o, axis=-1, keepdims=True)
    var = jnp.mean(jnp.square(o - mu), axis=-1, keepdims=True)
    o = ((o - mu) * lax.rsqrt(var + EPS)).reshape(B, S, RET_VW) * gn_g.astype(jnp.float32)
    y = (jax.nn.silu(g.astype(jnp.float32)) * o).astype(h.dtype)
    return y @ w_out

def _chunk_attention(h, w_in, rel_bias, w_out):
    B, S, _ = h.shape
    nc = S // CHUNK
    q, k, v = jnp.split(h @ w_in, 3, axis=-1)
    q = q.reshape(B, S, ATT_HEADS, ATT_DH)
    k = k.reshape(B, S, ATT_HEADS, ATT_DH)
    v = v.reshape(B, S, ATT_HEADS, ATT_DH)
    pad = ((0, 0), (BAND_PAST, 0), (0, 0), (0, 0))
    kp = jnp.pad(k, pad)
    vp = jnp.pad(v, pad)
    qi = jnp.arange(CHUNK)[:, None]
    kj = jnp.arange(BAND)[None, :]
    rel = kj - BAND_PAST - qi
    bidx = jnp.maximum(rel, -MAX_REL) + MAX_REL
    bias = rel_bias[:, bidx].astype(jnp.float32)
    scale = ATT_DH ** -0.5

    def one_chunk(c):
        start = c * CHUNK
        qb = lax.dynamic_slice_in_dim(q, start, CHUNK, axis=1)
        kb = lax.dynamic_slice_in_dim(kp, start, BAND, axis=1)
        vb = lax.dynamic_slice_in_dim(vp, start, BAND, axis=1)
        s = jnp.einsum('bqhd,bkhd->bhqk', qb, kb).astype(jnp.float32) * scale + bias[None]
        valid = (start - BAND_PAST + jnp.arange(BAND)) >= 0
        s = jnp.where(valid[None, None, None, :], s, -jnp.inf)
        p = jax.nn.softmax(s, axis=-1).astype(vb.dtype)
        return jnp.einsum('bhqk,bkhd->bqhd', p, vb)

    o = lax.map(one_chunk, jnp.arange(nc))
    o = o.transpose(1, 0, 2, 3, 4).reshape(B, S, ATT_HEADS * ATT_DH)
    return o @ w_out

def _sqrelu_mlp(h, w1, w2):
    u = jax.nn.relu(h @ w1)
    return (u * u) @ w2

def second_inputs(seed: int = 0) -> dict:
    key = jax.random.key(seed)
    ks = jax.random.split(key, 12)
    n_ret = (DEPTH_2 + 1) // 2
    n_att = DEPTH_2 // 2
    f = jnp.float32
    x = jax.random.normal(ks[0], (BATCH, SEQ, D_MODEL), f)
    mix_norm_g = 1.0 + 0.02 * jax.random.normal(ks[1], (DEPTH_2, D_MODEL), f)
    ret_w_in = jax.random.normal(ks[2], (n_ret, D_MODEL, 2 * RET_QK + 2 * RET_VW), f) * D_MODEL ** -0.5
    ret_gn_g = 1.0 + 0.02 * jax.random.normal(ks[3], (n_ret, RET_VW), f)
    ret_w_out = jax.random.normal(ks[4], (n_ret, RET_VW, D_MODEL), f) * RET_VW ** -0.5
    att_w_in = jax.random.normal(ks[5], (n_att, D_MODEL, 3 * D_MODEL), f) * D_MODEL ** -0.5
    att_rel_bias = 0.1 * jax.random.normal(ks[6], (n_att, ATT_HEADS, REL_TABLE), f)
    att_w_out = jax.random.normal(ks[7], (n_att, D_MODEL, D_MODEL), f) * D_MODEL ** -0.5
    mlp_norm_g = 1.0 + 0.02 * jax.random.normal(ks[8], (DEPTH_2, D_MODEL), f)
    mlp_w1 = jax.random.normal(ks[9], (DEPTH_2, D_MODEL, D_FF_2), f) * D_MODEL ** -0.5
    mlp_w2 = jax.random.normal(ks[10], (DEPTH_2, D_FF_2, D_MODEL), f) * D_FF_2 ** -0.5
    final_norm_g = 1.0 + 0.02 * jax.random.normal(ks[11], (D_MODEL,), f)
    return {"x": x, "mix_norm_g": mix_norm_g, "ret_w_in": ret_w_in, "ret_gn_g": ret_gn_g,
            "ret_w_out": ret_w_out, "att_w_in": att_w_in, "att_rel_bias": att_rel_bias,
            "att_w_out": att_w_out, "mlp_norm_g": mlp_norm_g, "mlp_w1": mlp_w1,
            "mlp_w2": mlp_w2, "final_norm_g": final_norm_g}

def second_block(x, mix_norm_g, ret_w_in, ret_gn_g, ret_w_out, att_w_in, att_rel_bias,
              att_w_out, mlp_norm_g, mlp_w1, mlp_w2, final_norm_g):
    h = x
    for i in range(DEPTH_2):
        hn = _rmsnorm(h, mix_norm_g[i])
        j = i // N_MIXERS
        if i % N_MIXERS == 0:
            h = h + _retention(hn, ret_w_in[j], ret_gn_g[j], ret_w_out[j])
        else:
            h = h + _chunk_attention(hn, att_w_in[j], att_rel_bias[j], att_w_out[j])
        h = h + _sqrelu_mlp(_rmsnorm(h, mlp_norm_g[i]), mlp_w1[i], mlp_w2[i])
    return _rmsnorm(h, final_norm_g)


def setup_inputs(seed=0):
    out = dict(first_inputs(seed))
    for name, value in second_inputs(seed + 1).items():
        if name != "x":
            out[name + "_2"] = value
    return out


def reference(
    x, norm_mix_g, w_in, conv_a_w, conv_b_w, conv_b_b, ln_b_g, ln_b_b, w_out, norm_ffn_g,
    w_gate, w_up, conv_ffn_w, w_down, norm_final_g, mix_norm_g_2, ret_w_in_2, ret_gn_g_2,
    ret_w_out_2, att_w_in_2, att_rel_bias_2, att_w_out_2, mlp_norm_g_2, mlp_w1_2, mlp_w2_2,
    final_norm_g_2,
):
    x = first_block(
        x, norm_mix_g, w_in, conv_a_w, conv_b_w, conv_b_b, ln_b_g, ln_b_b, w_out, norm_ffn_g,
        w_gate, w_up, conv_ffn_w, w_down, norm_final_g,
    )
    return second_block(
        x, mix_norm_g_2, ret_w_in_2, ret_gn_g_2, ret_w_out_2, att_w_in_2, att_rel_bias_2,
        att_w_out_2, mlp_norm_g_2, mlp_w1_2, mlp_w2_2, final_norm_g_2,
    )


_drawn_inputs = setup_inputs


def setup_inputs(seed=0):
    import zlib

    import numpy as np

    out = dict(_drawn_inputs(seed))
    spreads = {}
    factors = {'ln_b_b': 4.739,
     'ret_gn_g_2': 13.802,
     'att_rel_bias_2': 64.0,
     'mlp_norm_g_2': 4.615,
     'att_w_in_2': 3.485,
     'att_w_out_2': 3.43}
    for name, (base, spread) in spreads.items():
        noise = np.random.default_rng([zlib.crc32(name.encode()), seed]).standard_normal(out[name].shape)
        drawn = base * np.exp(spread * noise) if base else spread * noise
        out[name] = __import__('jax').numpy.asarray(drawn.astype(out[name].dtype))
    for name, factor in factors.items():
        out[name] = (out[name] * factor).astype(out[name].dtype)
    return out
```

```python
from contextlib import ExitStack

import concourse.bass as bass
from concourse import mybir
import numpy as np

F32 = mybir.dt.float32
F32R = mybir.dt.float32r
ALU = mybir.AluOpType
ACT = mybir.ActivationFunctionType

P = 128
SEQ = 512
D = 1024
KT = D // P
ST = SEQ // P
HALF = 128
FF = 2816
D_A = 512
TAPS = 31
PADC = TAPS // 2
UPW = SEQ + 2 * PADC
RET_HEADS = 4
ATT_HEADS = 16
MLP_CHUNKS = 4
EPS = 1e-6
LN_EPS = 1e-5
REL = 320
MASKED = -3.0e38

ROWS = {}
_at = 0
for _name, _n in (("norm_mix_g", 8), ("conv_a_w", 12), ("conv_b_b", 4), ("ln_b_g", 4), ("ln_b_b", 4),
                  ("norm_ffn_g", 8), ("norm_final_g", 8), ("mix_norm_g_2", 16), ("ret_gn_g_2", 16),
                  ("mlp_norm_g_2", 16), ("final_norm_g_2", 8), ("", 24), ("conv_b_w", 124), ("", 4),
                  ("conv_ffn_w", 66)):
    if _name:
        ROWS[_name] = (_at, _n)
    _at += _n
PROWS = 3
FILLED = (104, 124, 66)

BY_KEY = [0, 640, 1024, 512]
BY_QUERY = [0, 1024, 128, 512]
PACKED = 1280
TURNED = ((4, 0, 512), (5, 512, 512), (6, 1024, 256))
SCORES = {0: (2, 0), 2: (2, 128), 3: (3, 0), 1: (2, 0)}

K4_ORDER = [0, 2, 1, 3, 4, 6, 5, 7]
NATURAL = list(range(KT))


class Count:

    def __init__(self):
        self.n, self.turn, self.per = 0, None, 0

    def value(self, off=0):
        return self.n + off if self.turn is None else self.turn * self.per + (self.n + off)

    def beyond(self, k):
        return self.turn is not None or self.n > k


class Counts:

    def __init__(self, engine, sems):
        self.engine = engine
        self.of = {s: Count() for s in sems}
        self.block, self.unit = Count(), Count()
        self.latest = None

    def made(self, sem, k=1):
        self.of[sem].n += k
        self.latest = sem
        return k

    def next(self, sem, k=1):
        self.of[sem].n += k
        return self.of[sem].value()

    def now(self, sem):
        return self.of[sem].value()

    def own(self):
        return self.latest, self.of[self.latest].value()

    def repeat(self, turns, body):
        every = [*self.of.values(), self.block, self.unit]
        before = [x.n for x in every]
        body(0)
        per = [x.n - b for x, b in zip(every, before)]
        if turns == 1:
            return
        with self.engine.Fori(1, turns) as i:
            for x, b, p in zip(every, before, per):
                x.n, x.per, x.turn = b, p, i
            body(i)
        for x, b, p in zip(every, before, per):
            assert x.n - b == p
            x.n, x.turn = b + turns * p, None


def build(nc, phases, x_in, w_in, w_out, w_gate, w_up, w_down, ret_w_in, ret_w_out, att_w_in,
          att_w_out, w1, w2, rel_bias, params, consts, out):
    ident_c, cos_c, sin_c, decay_c = consts
    ctx = ExitStack()
    with ctx:
        def sb(name, shape, dt=F32):
            return ctx.enter_context(nc.sbuf_tensor(name, shape, dt))

        x = sb("x", [P, KT, SEQ])
        xh = sb("xh", [P, KT, SEQ], F32R)
        xl = sb("xl", [P, KT, SEQ], F32R)
        hh = sb("hid_hi", [P, KT, SEQ], F32R)
        hl = sb("hid_lo", [P, KT, SEQ], F32R)
        raw = sb("raw", [P, 2, 2048])
        wh = sb("w_hi", [P, 2, 2048], F32R)
        wl = sb("w_lo", [P, 2, 2048], F32R)
        qh = sb("q_hi", [P, 2, SEQ], F32R)
        ql = sb("q_lo", [P, 2, SEQ], F32R)
        kh = sb("k_hi", [P, 2, SEQ], F32R)
        kl = sb("k_lo", [P, 2, SEQ], F32R)
        avh = sb("att_v_hi", [P, ST, 256], F32R)
        avl = sb("att_v_lo", [P, ST, 256], F32R)
        pth = sb("probs_t_hi", [P, PACKED], F32R)
        ptl = sb("probs_t_lo", [P, PACKED], F32R)
        work = sb("work", [P, 8448])
        r_bc = sb("r_bc", [P, SEQ])
        ssq = sb("ssq", [P, SEQ])
        sq = sb("sq", [P, SEQ])
        ident = sb("ident", [P, P])
        ones = sb("ones", [P, P])
        prm = sb("prm", [P, PROWS * P])
        cols = sb("cols", [P, 64])
        ps = ctx.enter_context(nc.psum_tensor("ps", [P, 8, SEQ], F32))
        bias_dram = nc.dram_tensor("bias_by_query", (ATT_HEADS, P, SEQ), F32).ap()

        diag = sq[:, :].rearrange("p (i c) -> p i c", i=ST)
        ms, root, rc, t4 = (cols[:, 4 * k:4 * k + 4] for k in range(4))
        ms2, r1c = cols[:, 16:20], cols[:, 20:24]
        mv = cols[:, 24:32].rearrange("p (i c) -> p i c", c=2)
        mx, nmx, rs, rinv = (cols[:, 32 + 4 * k:36 + 4 * k] for k in range(4))
        bn = cols[:, 48:54]

        def part(at, *shape):
            n = int(np.prod(shape))
            v = work[:, at:at + n]
            return v if len(shape) == 1 else v.rearrange("p (a b) -> p a b", a=shape[0])

        upad, cacc, apad, gbuf, ybuf = (part(0, 4, UPW), part(2168, 4, SEQ), part(4216, 4, SEQ + 2),
                                        part(6272, 2, SEQ), part(7296, 2, SEQ))
        x_rows, p_rows = part(4216, ST, D), part(2808, PROWS, P)
        ext = work[0:ATT_HEADS, 2168:2808]
        gpad, gconv, gact, hval = part(3072, 2, SEQ + 2), part(4100, 2, SEQ), part(5124, 2, SEQ), part(6148, 2, SEQ)
        cos, sin, decay = part(0, SEQ), part(512, SEQ), part(1024, RET_HEADS, SEQ)
        sg, o_sb, ptf = part(3072, 4, SEQ), part(5120, ST, SEQ), part(7168, PACKED)
        bias, probs = part(0, 4, SEQ), part(2048, 2, PACKED)

        def prow(name, r):
            at, n = ROWS[name]
            assert r < n if isinstance(r, int) else True
            if isinstance(r, int):
                return prm[:, at + r:at + r + 1]
            return prm[:, bass.ds(r + at, 1)]

        sems = []

        def sem(name):
            sems.append(ctx.enter_context(nc.semaphore(name)))
            return sems[-1]

        w_landed = [sem(f"w_landed{i}") for i in range(2)]
        bias_landed = [sem(f"bias_landed{i}") for i in range(4)]
        w_hi = sem("w_hi")
        w_lo = sem("w_lo")
        unit_done = sem("unit_done")
        unit_taken = sem("unit_taken")
        x_added = sem("x_added")
        x_ready = sem("x_ready")
        hid_ready = sem("hid_ready")
        hi_made = sem("hi_made")
        curve_made = sem("curve_made")
        to_hi = sem("to_hi")
        to_curve = sem("to_curve")
        stats_in = sem("stats_in")
        stats_done = sem("stats_done")
        turned = sem("turned")
        scores_done = sem("scores_done")
        mixed_done = sem("mixed_done")
        qk_ready = sem("qk_ready")
        pt_ready = sem("pt_ready")
        p_ready = sem("p_ready")
        s_taken = sem("s_taken")
        o_taken = sem("o_taken")
        dve_step = sem("dve_step")
        x_landed = sem("x_landed")
        p_landed = sem("p_landed")
        c_landed = sem("c_landed")
        ext_landed = sem("ext_landed")
        ext_built = sem("ext_built")
        ext_stored = sem("ext_stored")
        tab_landed = sem("tab_landed")
        out_ready_act = sem("out_ready_act")
        out_ready_dve = sem("out_ready_dve")
        out_stored = sem("out_stored")
        ones_set = sem("ones_set")
        prm_ready = sem("prm_ready")
        rc_final = sem("rc_final")
        act_step = sem("act_step")

        x_added_total = KT * (1 + len(phases))
        turned_before_att = 1 + KT + (4 * RET_HEADS if "ret" in phases else 0)
        turned_total = turned_before_att + (len(TURNED) * ATT_HEADS if "att" in phases else 0)
        block = ctx.enter_context(nc.Block())

        n_blocks = sum({"mix": 14, "ffn": 34, "ret": 32, "mlp0": 32, "att": 16, "mlp1": 32}[f] for f in phases)

        def next_prep(f):
            k = phases.index(f) + 1
            if k == len(phases):
                return ("final", "final_norm_g_2", 0)
            return {"ffn": ("norm", "norm_ffn_g", 0), "ret": ("double", "mix_norm_g_2", 0),
                    "mlp0": ("norm", "mlp_norm_g_2", 0), "att": ("norm", "mix_norm_g_2", 8),
                    "mlp1": ("norm", "mlp_norm_g_2", 8)}[phases[k]]

        @block.sync
        def _(sp):
            c = Counts(sp, sems)

            def load(matrix, k0, nk, c0, width):
                slot = c.block.n % 2
                if c.block.beyond(1):
                    sp.wait_ge(w_lo, 2 * c.block.value(-1))
                dst = raw[:, slot, 0:nk * width].rearrange("p (k c) -> p k c", k=nk)
                rows = slice(k0, k0 + nk) if isinstance(k0, int) else bass.ds(k0, nk)
                wide = slice(c0, c0 + width) if isinstance(c0, int) else bass.ds(c0, width)
                src = matrix.rearrange("(k p) f -> p k f", p=P)[:, rows, wide]
                sp.dma_start(dst, src).then_inc(w_landed[slot], c.made(w_landed[slot], 16))
                c.block.n += 1

            for v, (lo, hi) in params:
                t, at = divmod(lo, P)
                sp.dma_start(p_rows[at:at + hi - lo, t, :], v).then_inc(p_landed, 16)
            sp.dma_start(x_rows, x_in.rearrange("(s p) d -> p s d", p=P)).then_inc(x_landed, 16)

            def outs_k4(matrix, k0):
                for b in range(2):
                    load(matrix, k0, 4, 512 * b, 512)

            def outs_k8(matrix, k0, nk=KT):
                for b in range(4):
                    load(matrix, k0, nk, 256 * b, 256)

            for f in phases:
                if f == "mix":
                    for j in range(2):
                        load(w_in, 0, KT, 3 * D_A + 256 * j, 256)
                        load(w_in, 0, KT, 4 * D_A + 256 * j, 256)
                    for c0 in (0, 2 * D_A, D_A):
                        for j in range(2):
                            load(w_in, 0, KT, c0 + 256 * j, 256)
                    outs_k4(w_out, 0)
                    outs_k4(w_out, 4)
                if f == "ffn":
                    def chunk(i, tiles=8):
                        for b in range(tiles // 2):
                            load(w_gate, 0, KT, i * 1024 + 256 * b, 256)
                            load(w_up, 0, KT, i * 1024 + 256 * b, 256)
                        outs_k8(w_down, i * 8, tiles)
                    c.repeat(2, chunk)
                    chunk(2, 6)
                if f == "ret":
                    def head(h):
                        load(ret_w_in, 0, KT, h * 256, 256)
                        load(ret_w_in, 0, KT, h * 256 + 1024, 256)
                        for c0 in (2048, 2304, 4096, 4352):
                            load(ret_w_in, 0, KT, h * 512 + c0, 256)
                        outs_k4(ret_w_out, h * 4)
                    c.repeat(RET_HEADS, head)
                if f == "att":
                    def group(g):
                        for c0 in (0, 1024, 2048):
                            load(att_w_in, 0, KT, g * 256 + c0, 256)
                    def group_pair(gp):
                        group(gp * 2)
                        group(gp * 2 + 1)
                    c.repeat(2, group_pair)
                    outs_k8(att_w_out, 0)
                if f in ("mlp0", "mlp1"):
                    m = int(f[-1])
                    def chunk(i, m=m):
                        for b in range(4):
                            load(w1[m], 0, KT, i * 1024 + 256 * b, 256)
                        outs_k8(w2[m], i * 8)
                    c.repeat(MLP_CHUNKS, chunk)
            assert c.block.n == n_blocks
            for i in range(ST):
                sp.wait_ge(out_ready_act, i + 1)
                sp.wait_ge(out_ready_dve, i + 1)
                sp.dma_start(out[i * P:(i + 1) * P, :], work[:, i * D:(i + 1) * D]).then_inc(out_stored, 16)
            sp.wait_ge(out_stored, 16 * ST)

        @block.gpsimd
        def _(pool):
            c = Counts(pool, sems)
            nc.gpsimd.memset(ones[:, :], 1.0).then_inc(ones_set, 1)

            def pair(i):
                for slot in range(2):
                    for half in range(2):
                        pool.wait_ge(w_hi, c.next(w_hi))
                        cut = (slice(None), slot, slice(None), slice(HALF * half, HALF * (half + 1)))
                        view = [t[:, :, :].rearrange("p s (k c) -> p s k c", c=256)[cut] for t in (wl, raw, wh)]
                        nc.gpsimd.tensor_tensor(view[0], view[1], view[2].bitcast(F32), ALU.subtract).then_inc(w_lo, c.made(w_lo))
            c.repeat(n_blocks // 2, pair)

        @block.tensor
        def _(pe):
            c = Counts(pe, sems)
            banks = [4]

            def product(o, a, b, first, last):
                nc.tensor.matmul(o, a[0], b[0], start=first, stop=False, skip_group_check=True)
                nc.tensor.matmul(o, a[0], b[1], start=False, stop=False, skip_group_check=True)
                return nc.tensor.matmul(o, a[1], b[0], start=False, stop=last, skip_group_check=True)

            def weights(slot, width):
                return [t[:, slot, :].rearrange("p (k c) -> p k c", c=width) for t in (wh, wl)]

            def unit8(rhs, nk=KT, order=None, ready=None, fresh=False, slot=None, half=None, ahead=1):
                slot = c.unit.n // 2 % 2 if slot is None else slot
                half = c.unit.n % 2 if half is None else half
                pe.wait_ge(w_lo, c.unit.value(ahead))
                others = 0 if fresh else banks[0] - 1
                if c.unit.beyond(others):
                    pe.wait_ge(unit_taken, c.unit.value(-others))
                w = weights(slot, 256)
                order = order or list(range(nk))
                for n, k in enumerate(order):
                    if ready:
                        pe.wait_ge(ready, c.next(ready))
                    a = [t[:, k, HALF * half:HALF * (half + 1)] for t in w]
                    mm = product(ps[:, c.unit.n % banks[0], :], a, [t[:, k, :] for t in rhs], n == 0, n == nk - 1)
                mm.then_inc(unit_done, c.made(unit_done))
                c.unit.n += 1

            def unit4(rhs, k0, ready=None, fresh=False):
                slot, half = c.unit.n // 2 % 2, c.unit.n % 2
                pe.wait_ge(w_lo, c.unit.value(1))
                pe.wait_ge(unit_taken, c.unit.value(0 if fresh else -1))
                w = weights(slot, 512)
                for m in range(2):
                    for k in range(4):
                        if ready and m == 0:
                            pe.wait_ge(ready, c.next(ready))
                        f = half + 2 * m
                        a = [t[:, k, P * f:P * (f + 1)] for t in w]
                        mm = product(ps[:, 2 * half + m, :], a, [t[:, k0 + k, :] for t in rhs], k == 0, k == 3)
                mm.then_inc(unit_done, c.made(unit_done))
                c.unit.n += 1

            def unit_v(lhs):
                slot, half = c.unit.n // 2 % 2, c.unit.n % 2
                pe.wait_ge(w_lo, c.unit.value(2 - half))
                pe.wait_ge(unit_taken, c.unit.value(1 - banks[0]))
                w = weights(slot, 256)
                for m in range(2):
                    s = 2 * half + m
                    for k in range(KT):
                        a = [t[:, k, P * s:P * (s + 1)] for t in lhs]
                        mm = product(ps[:, c.unit.n % banks[0], 256 * m:256 * (m + 1)], a, [t[:, k, :] for t in w],
                                     k == 0, k == KT - 1)
                mm.then_inc(unit_done, c.made(unit_done))
                c.unit.n += 1

            def column_sums(src, col=0):
                for i in range(ST):
                    mm = nc.tensor.matmul(ps[:, 4, col + i:col + i + 1], src[:, P * i:P * (i + 1)], ones[:, 0:1],
                                          start=True, stop=True, skip_group_check=True)
                return mm

            def stats(second=None):
                pe.wait_ge(stats_in, c.next(stats_in))
                mm = column_sums(ssq)
                if second is not None:
                    mm = column_sums(second, 4)
                mm.then_inc(stats_done, c.made(stats_done))

            def spread():
                pe.wait_ge(stats_in, c.next(stats_in))
                for i in range(ST):
                    mm = nc.tensor.matmul(ps[:, 5, P * i:P * (i + 1)], ones[:, :], diag[:, i, :],
                                          start=True, stop=True, skip_group_check=True)
                mm.then_inc(stats_done, c.made(stats_done))

            X, H = (xh, xl), (hh, hl)

            pe.wait_ge(c_landed, 16)
            pe.wait_ge(p_landed, 16 * len(params))
            for t in range(PROWS):
                n = FILLED[t]
                mm = nc.tensor.transpose(ps[:, 0, P * t:P * t + n], p_rows[0:n, t, :], ident[0:n, 0:n])
            mm.then_inc(turned, c.made(turned))
            pe.wait_ge(x_landed, 16)
            for d in range(KT):
                if d == KT - 1:
                    pe.wait_ge(prm_ready, PROWS)
                for s in range(ST):
                    mm = nc.tensor.transpose(ps[:, (d + 1) % 8, P * s:P * (s + 1)],
                                             x_rows[:, s, P * d:P * (d + 1)], ident[:, :])
                mm.then_inc(turned, c.made(turned))
            pe.wait_ge(ones_set, 1)

            def first_units(order, double=False):
                unit8(X, order=order, ready=x_ready, fresh=True)
                stats(r_bc if double else None)
                unit8(X)
                spread()

            order = NATURAL
            for f in phases:
                if f == "mix":
                    pe.wait_ge(x_added, KT)
                    first_units(order)
                    for _ in range(2, 20):
                        unit8(X)
                    unit4(H, 0, ready=hid_ready, fresh=True)
                    stats()
                    unit4(H, 0)
                    spread()
                    unit4(H, 0)
                    stats()
                    unit4(H, 0)
                    spread()
                    unit4(H, 4, ready=hid_ready)
                    for _ in range(3):
                        unit4(H, 4)
                    order = K4_ORDER
                if f == "ffn":
                    def chunk(i, tiles=8, first=False):
                        if first:
                            first_units(order)
                        for _ in range(2 if first else 0, 2 * tiles):
                            unit8(X)
                        unit8(H, tiles, ready=hid_ready)
                        for _ in range(7):
                            unit8(H, tiles)
                    chunk(0, first=True)
                    chunk(1)
                    chunk(2, 6)
                    order = NATURAL
                if f == "ret":
                    def head(h, first=False):
                        if first:
                            first_units(order, double=True)
                            spread()
                        else:
                            unit8(X, fresh=True)
                            unit8(X)
                        unit8(X)
                        unit8(X)
                        for _ in range(3):
                            unit_v(X)
                        pe.wait_ge(qk_ready, c.next(qk_ready, 2))
                        for j in range(ST):
                            n = SEQ - P * j
                            for t in range(2):
                                mm = product(ps[:, 4 + j, 0:n], [v[:, t, P * j:P * (j + 1)] for v in (kh, kl)],
                                             [v[:, t, P * j:SEQ] for v in (qh, ql)], t == 0, t == 1)
                            mm.then_inc(scores_done, c.made(scores_done))
                        unit_v(X)
                        unit8(X)
                        pe.wait_ge(unit_taken, c.unit.value(-1))
                        pe.wait_ge(pt_ready, c.next(pt_ready, 4))
                        for i in range(ST):
                            if i >= 2:
                                pe.wait_ge(o_taken, c.next(o_taken))
                            for j in range(i + 1):
                                at = BY_KEY[j] + P * (i - j)
                                mm = product(ps[:, 6 + i % 2, :], [v[:, at:at + P] for v in (pth, ptl)],
                                             [v[:, 4 + j, :] for v in (hh, hl)], j == 0, j == i)
                            mm.then_inc(mixed_done, c.made(mixed_done))
                        unit8(X)
                        unit8(X)
                        pe.wait_ge(o_taken, c.next(o_taken, 2))
                        pe.wait_ge(p_ready, c.next(p_ready, 4))
                        for j in range(4):
                            for i in range(ST):
                                mm = nc.tensor.transpose(ps[:, 4 + j, P * i:P * (i + 1)],
                                                         o_sb[:, i, P * j:P * (j + 1)], ident[:, :])
                            mm.then_inc(turned, c.made(turned))
                        unit8(X)
                        unit4(H, 0, ready=hid_ready, fresh=True)
                        for _ in range(3):
                            unit4(H, 0)
                    head(0, True)
                    c.repeat(RET_HEADS - 1, head)
                    order = K4_ORDER
                if f in ("mlp0", "mlp1"):
                    def chunk(i, first=False):
                        if first:
                            first_units(order)
                        for _ in range(2 if first else 0, 8):
                            unit8(X)
                        unit8(H, ready=hid_ready)
                        for _ in range(7):
                            unit8(H)
                    chunk(0, True)
                    c.repeat(MLP_CHUNKS - 1, chunk)
                    order = NATURAL
                if f == "att":
                    banks[0] = 2

                    def qk_unit(n, fresh=False):
                        slot0 = (c.unit.n - n) // 2 % 2
                        unit8(X, slot=(slot0 + n % 2) % 2, half=n // 2, ahead=(1, 2, 0, 1)[n], fresh=fresh)

                    def scores(h):
                        if h % 2 == 0:
                            pe.wait_ge(qk_ready, c.next(qk_ready, 2))
                        t, rows = h % 4 // 2, slice(64 * (h % 2), 64 * (h % 2) + 64)
                        for i, (bank, at) in SCORES.items():
                            n = P * (i + 1)
                            if i == 0 and h:
                                pe.wait_ge(s_taken, ST * h)
                            if i == 1:
                                pe.wait_ge(s_taken, ST * h + 2)
                            mm = product(ps[:, bank, at:at + n], [v[rows, t, P * i:P * (i + 1)] for v in (qh, ql)],
                                         [v[rows, t, 0:n] for v in (kh, kl)], True, True)
                            if i != 0:
                                mm.then_inc(scores_done, c.made(scores_done))

                    def turn(h):
                        pe.wait_ge(p_ready, c.next(p_ready))
                        for bank, at, n in TURNED:
                            for j in range(ST):
                                if not at <= BY_KEY[j] < at + n:
                                    continue
                                for i in range(j, ST):
                                    src = BY_QUERY[i] + P * j
                                    o = BY_KEY[j] - at + P * (i - j)
                                    mm = nc.tensor.transpose(ps[:, bank, o:o + P], probs[:, h % 2, src:src + P], ident[:, :])
                            mm.then_inc(turned, c.made(turned))

                    def mix(h):
                        if h:
                            pe.wait_ge(hid_ready, c.next(hid_ready))
                        pe.wait_ge(pt_ready, c.next(pt_ready, len(TURNED)))
                        for j in range(ST):
                            t = h % 4 // 2
                            n = SEQ - P * j
                            mm = product(ps[:, 7, P * j:SEQ], [v[:, j, P * t:P * (t + 1)] for v in (avh, avl)],
                                         [v[:, BY_KEY[j]:BY_KEY[j] + n] for v in (pth, ptl)], j == 0, j == ST - 1)
                        mm.then_inc(mixed_done, c.made(mixed_done))

                    unit8(X, order=order, ready=x_ready, fresh=True)
                    stats()
                    qk_unit(1)
                    spread()
                    qk_unit(2)
                    qk_unit(3)
                    scores(0)
                    for h in range(ATT_HEADS):
                        s, more = h % 4, h < ATT_HEADS - 4
                        if h + 1 < ATT_HEADS:
                            scores(h + 1)
                        if s == 0:
                            if h:
                                mix(h - 1)
                            unit_v(X)
                            turn(h)
                            unit_v(X)
                            v_units = c.unit.n
                            continue
                        if more:
                            qk_unit((0, 0, 2, 3)[s])
                        if s == 1:
                            pe.wait_ge(unit_taken, v_units)
                        mix(h - 1)
                        turn(h)
                        if s == 1 and more:
                            qk_unit(1)
                    mix(ATT_HEADS - 1)
                    banks[0] = 4
                    pe.wait_ge(hid_ready, c.next(hid_ready, 1))
                    unit8(H, fresh=True)
                    for _ in range(7):
                        unit8(H)
                    order = NATURAL

            pe.wait_ge(stats_in, c.next(stats_in))
            column_sums(ssq).then_inc(stats_done, c.made(stats_done))
            pe.wait_ge(unit_taken, c.unit.n)
            pe.wait_ge(x_added, x_added_total)
            for n in range(8):
                i, half = divmod(n, 2)
                bank = (0, 1, 2, 3, 5, 6, 7, 4)[n]
                if bank == 4:
                    pe.wait_ge(rc_final, 1)
                for d in range(4):
                    mm = nc.tensor.transpose(ps[:, bank, P * d:P * (d + 1)], x[:, 4 * half + d, P * i:P * (i + 1)],
                                             ident[:, :])
                mm.then_inc(turned, c.made(turned))


        @block.scalar
        def _(act):
            c = Counts(act, sems)
            act.dma_start(ident[:, :], ident_c).then_inc(c_landed, 16)
            act.dma_start(ext[:, 255:575], rel_bias).then_inc(ext_landed, 16)

            def convert(n=1):
                for _ in range(n):
                    place = c.of[w_hi]
                    halves = place.n
                    if place.turn is None and halves >= 2 * n_blocks:
                        return
                    slot, half = halves // 2 % 2, halves % 2
                    act.wait_ge(w_landed[slot], place.value(-(halves % 4)) * 4 + 16)
                    cut = (slice(None), slot, slice(None), slice(HALF * half, HALF * (half + 1)))
                    view = [t[:, :, :].rearrange("p s (k c) -> p s k c", c=256)[cut] for t in (wh, raw)]
                    nc.scalar.activation(view[0], view[1], ACT.Copy).then_inc(w_hi, c.made(w_hi))

            def after_unit():
                act.wait_ge(unit_done, c.next(unit_done))
                c.unit.n += 1
                convert()

            def make_root():
                act.wait_ge(to_curve, c.next(to_curve))
                nc.scalar.activation(root, ms, ACT.Sqrt).then_inc(curve_made, c.made(curve_made))

            def hi_of(dst, src):
                act.wait_ge(to_hi, c.next(to_hi))
                nc.scalar.activation(dst, src, ACT.Copy).then_inc(hi_made, c.made(hi_made))

            def prep(d, kind, name, row):
                act.wait_ge(x_added, c.next(x_added))
                if kind != "final":
                    nc.scalar.activation(xh[:, d, :], x[:, d, :], ACT.Copy, scale=prow(name, row + d)).then_inc(hi_made, c.made(hi_made))

            def out_units8(prepare=None):
                for d in range(KT):
                    if prepare:
                        prep(d, *prepare)
                    after_unit()

            def out_units4(prepare=None):
                for b in range(2):
                    for half in range(2):
                        for m in range(2):
                            if prepare:
                                prep(4 * b + half + 2 * m, *prepare)
                        after_unit()

            def taken():
                act.wait_ge(unit_taken, c.unit.value(1))

            def value_hi(dst, c0):
                act.wait_ge(unit_done, c.unit.value(1))
                u, half = c.unit.n, c.unit.n % 2
                for m in range(2):
                    s = 2 * half + m
                    last = nc.scalar.activation(dst[:, s, c0:c0 + 256], ps[:, u % banks[0], 256 * m:256 * (m + 1)],
                                                ACT.Copy, scale=rc[:, s:s + 1])
                last.then_inc(hi_made, c.made(hi_made))

            def load_bias(h):
                for p0, n in ((0, 448), (64, SEQ)):
                    act.dma_start(bias[p0:p0 + 64, h % 4, 0:n], bias_dram[h, p0:p0 + 64, 0:n]).then_inc(bias_landed[h % 4], 16)

            banks = [4]
            act.wait_ge(ext_built, 1)
            rows = ext[:, 0:SEQ]
            skewed = bass.AP(rows.tensor, rows.offset + P - 1, [rows.ap[0], [-1, P], [1, SEQ]])
            act.dma_start(bias_dram, skewed).then_inc(ext_stored, 16)
            convert(4)
            for d in range(KT):
                prep(d, "norm", "norm_mix_g", 0)
            for f in phases:
                nxt = next_prep(f)
                if f == "mix":
                    make_root()
                    for u in range(20):
                        if u in (2, 3, 6, 7):
                            t = u % 2
                            taken()
                            nc.scalar.activation(gbuf[:, t, :], gbuf[:, t, :], ACT.Sigmoid).then_inc(curve_made, c.made(curve_made))
                        if u >= 16:
                            hi_of(hh[:, u - 16, :], ybuf[:, u % 2, :])
                        after_unit()
                    after_unit()
                    after_unit()
                    after_unit()
                    make_root()
                    after_unit()
                    for t in range(4):
                        act.wait_ge(to_curve, c.next(to_curve))
                        nc.scalar.activation(cacc[:, t, :], cacc[:, t, :], ACT.Silu, scale=prow("ln_b_g", t),
                                                   bias=prow("ln_b_b", t)).then_inc(act_step, c.made(act_step))
                        act.wait_ge(*c.own())
                        nc.scalar.activation(hh[:, 4 + t, :], cacc[:, t, :], ACT.Copy).then_inc(hi_made, c.made(hi_made))
                    out_units4(nxt)
                if f == "ffn":
                    for dst, src in ((cos, cos_c), (sin, sin_c), (decay, decay_c)) if "ret" in phases else ():
                        act.dma_start(dst, src).then_inc(tab_landed, 16)
                    def chunk(i, tiles=8, prepare=None):
                        for b in range(tiles // 2):
                            for t in range(2):
                                act.wait_ge(to_curve, c.next(to_curve))
                                nc.scalar.activation(gact[:, t, :], gconv[:, t, :], ACT.Silu).then_inc(curve_made, c.made(curve_made))
                                after_unit()
                            for t in range(2):
                                hi_of(hh[:, 2 * b + t, :], hval[:, t, :])
                                after_unit()
                        out_units8(prepare)
                    make_root()
                    chunk(0)
                    chunk(1)
                    chunk(2, 6, nxt)
                if f == "ret":
                    def head(h, prepare=None):
                        for dst in (qh, kh):
                            hi_of(dst[:, :, :], sg[:, 0:2, :])
                            after_unit()
                            after_unit()

                        def v_unit(n):
                            value_hi(hh[:, 4:8, :], 256 * (n // 2))
                            act.wait_ge(unit_done, c.next(unit_done))
                            c.unit.n += 1
                            if n % 2:
                                convert(2)
                        for n in range(3):
                            v_unit(n)
                        for j in range(ST):
                            act.wait_ge(to_hi, c.next(to_hi))
                            cut = slice(BY_KEY[j], BY_KEY[j] + SEQ - P * j)
                            nc.scalar.activation(pth[:, cut], ptf[:, cut], ACT.Copy).then_inc(hi_made, c.made(hi_made))
                        v_unit(3)

                        def gate(j):
                            taken()
                            nc.scalar.activation(sg[:, j, :], sg[:, j, :], ACT.Silu).then_inc(curve_made, c.made(curve_made))
                            after_unit()
                        gate(0)
                        for i in range(ST):
                            act.wait_ge(mixed_done, c.next(mixed_done))
                            nc.scalar.activation(o_sb[:, i, :], ps[:, 6 + i % 2, :], ACT.Copy).then_inc(curve_made, c.made(curve_made))
                        make_root()
                        gate(1)
                        gate(2)
                        for j in range(3):
                            hi_of(hh[:, j, :], sg[:, j, :])
                        gate(3)
                        hi_of(hh[:, 3, :], sg[:, 3, :])
                        out_units4(prepare)
                    make_root()
                    make_root()
                    head(0)
                    head(1)
                    head(2)
                    head(3, nxt)
                if f in ("mlp0", "mlp1"):
                    if f == "mlp0" and "att" in phases:
                        act.wait_ge(ext_stored, 16)
                        for h in range(4):
                            load_bias(h)
                    def chunk(i, prepare=None):
                        for u in range(8):
                            hi_of(hh[:, u, :], hval[:, u % 2, :])
                            after_unit()
                        out_units8(prepare)
                    make_root()
                    c.repeat(MLP_CHUNKS - 1, chunk)
                    chunk(MLP_CHUNKS - 1, nxt)
                if f == "att":
                    banks[0] = 2
                    make_root()

                    def qk_unit(n):
                        taken()
                        dst = (qh, kh)[n % 2]
                        nc.scalar.activation(dst[:, n // 2, :], hval[:, n % 2, :], ACT.Copy).then_inc(hi_made, c.made(hi_made))
                        act.wait_ge(unit_done, c.next(unit_done))
                        c.unit.n += 1
                        convert((1, 0, 1, 2)[n])

                    def v_unit(n):
                        value_hi(avh, 0)
                        act.wait_ge(unit_done, c.next(unit_done))
                        c.unit.n += 1
                        if n:
                            convert(2)

                    def exps(h):
                        act.wait_ge(to_curve, c.next(to_curve))
                        for i in range(ST):
                            cut = slice(BY_QUERY[i], BY_QUERY[i] + P * (i + 1))
                            last = nc.scalar.activation(probs[:, h % 2, cut], probs[:, h % 2, cut], ACT.Exp,
                                                        bias=nmx[:, i:i + 1], accum_out=rs[:, i:i + 1])
                        last.then_inc(curve_made, c.made(curve_made))
                        if h + 4 < ATT_HEADS:
                            load_bias(h + 4)

                    def probs_hi():
                        for bank, at, n in TURNED:
                            act.wait_ge(turned, c.next(turned))
                            nc.scalar.activation(pth[:, at:at + n], ps[:, bank, 0:n], ACT.Copy).then_inc(hi_made, c.made(hi_made))

                    def mixed_hi(h):
                        rows = slice(64 * (h % 2), 64 * (h % 2) + 64)
                        act.wait_ge(mixed_done, c.next(mixed_done))
                        nc.scalar.activation(hh[rows, h // 2, :], ps[rows, 7, :], ACT.Copy).then_inc(hi_made, c.made(hi_made))

                    for n in range(4):
                        qk_unit(n)
                    c.of[turned].n = turned_before_att
                    exps(0)
                    for h in range(ATT_HEADS):
                        s, more = h % 4, h < ATT_HEADS - 4
                        if h + 1 < ATT_HEADS:
                            exps(h + 1)
                        if s == 0:
                            if h:
                                mixed_hi(h - 1)
                            v_unit(0)
                            probs_hi()
                            v_unit(1)
                            continue
                        if more:
                            qk_unit((0, 0, 2, 3)[s])
                        mixed_hi(h - 1)
                        probs_hi()
                        if s == 1 and more:
                            qk_unit(1)
                    mixed_hi(ATT_HEADS - 1)
                    banks[0] = 4
                    out_units8(nxt)
            make_root()
            act.wait_ge(rc_final, 1)
            for i in range(ST):
                act.wait_ge(turned, turned_total + 2 * i + 1)
                nc.scalar.activation(work[:, i * D:i * D + 512], ps[:, (0, 2, 5, 7)[i], :], ACT.Copy,
                                     scale=rc[:, i:i + 1]).then_inc(out_ready_act, 1)

        @block.vector
        def _(dve):
            c = Counts(dve, sems)
            V = nc.vector
            banks = [4]

            def bank():
                return ps[:, c.unit.n % banks[0], :]

            def refine(signal=dve_step):
                dve.wait_ge(curve_made, c.next(curve_made))
                V.reciprocal(rc, root).then_inc(dve_step, c.made(dve_step))
                dve.wait_ge(dve_step, c.now(dve_step))
                V.tensor_tensor(t4, rc, rc, ALU.mult).then_inc(dve_step, c.made(dve_step))
                dve.wait_ge(dve_step, c.now(dve_step))
                V.tensor_tensor(t4, t4, ms, ALU.mult).then_inc(dve_step, c.made(dve_step))
                dve.wait_ge(dve_step, c.now(dve_step))
                V.tensor_scalar(t4, t4, -0.5, 1.5, ALU.mult, ALU.add).then_inc(dve_step, c.made(dve_step))
                dve.wait_ge(dve_step, c.now(dve_step))
                V.tensor_tensor(rc, rc, t4, ALU.mult).then_inc(signal, c.made(signal))
                dve.wait_ge(signal, c.now(signal))

            def mean_square(n, eps):
                V.tensor_scalar(ms, ps[:, 4, 0:ST], 1.0 / n, eps, ALU.mult, ALU.add).then_inc(to_curve, c.made(to_curve))

            def diagonals(col):
                for i in range(ST):
                    V.tensor_scalar(diag[:, i, :], ident[:, :], col[:, i:i + 1], None, ALU.mult).then_inc(
                        dve_step if i < ST - 1 else stats_in, c.made(dve_step if i < ST - 1 else stats_in))
                dve.wait_ge(stats_done, c.next(stats_done))

            def factor():
                dve.wait_ge(stats_done, c.next(stats_done))
                mean_square(D, EPS)
                refine()
                diagonals(rc)
                V.tensor_copy(r_bc[:, :], ps[:, 5, :]).then_inc(dve_step, c.made(dve_step))
                dve.wait_ge(dve_step, c.now(dve_step))

            def square(d, signal):
                dve.wait_ge(*c.own())
                V.tensor_tensor(sq[:, :], x[:, d, :], x[:, d, :], ALU.mult).then_inc(signal, c.made(signal))
                dve.wait_ge(signal, c.now(signal))

            def add_square(total, first, signal=dve_step):
                if first:
                    V.tensor_copy(total[:, :], sq[:, :]).then_inc(signal, c.made(signal))
                else:
                    V.tensor_tensor(total[:, :], total[:, :], sq[:, :], ALU.add).then_inc(signal, c.made(signal))

            def input_lo(d, name, row):
                dve.wait_ge(hi_made, c.next(hi_made))
                V.scalar_tensor_tensor(xl[:, d, :], x[:, d, :], prow(name, row + d), xh[:, d, :].bitcast(F32),
                                       ALU.mult, ALU.subtract).then_inc(x_ready, c.made(x_ready))

            def finish_tile(d, before, last, prepare, unit_ends):
                kind, name, row = prepare
                first = before is None
                signal = unit_taken if unit_ends else dve_step
                square(d, signal)
                if kind == "final":
                    add_square(ssq, first, stats_in if last else dve_step)
                    V.tensor_scalar(x[:, d, :], x[:, d, :], prow(name, d), None, ALU.mult).then_inc(x_added, c.made(x_added))
                    return
                if kind == "double":
                    add_square(ssq, first)
                    V.tensor_scalar(x[:, d, :], x[:, d, :], prow("norm_final_g", d), None, ALU.mult).then_inc(
                        x_added, c.made(x_added))
                    square(d, dve_step)
                    add_square(r_bc, first, stats_in if last else dve_step)
                else:
                    add_square(ssq, first, stats_in if last else dve_step)
                if not first:
                    input_lo(before, name, row)
                if last:
                    input_lo(d, name, row)

            def sum_signal(prepare, otherwise):
                return x_added if prepare and prepare[0] == "norm" else dve_step if prepare else otherwise

            def out_units8(prepare=None):
                for d in range(KT):
                    dve.wait_ge(unit_done, c.next(unit_done))
                    signal = sum_signal(prepare, unit_taken)
                    V.tensor_tensor(x[:, d, :], x[:, d, :], bank(), ALU.add).then_inc(signal, c.made(signal))
                    if prepare:
                        finish_tile(d, d - 1 if d else None, d == KT - 1, prepare, True)
                    c.unit.n += 1

            def out_units4(prepare=None, between=None):
                for n, d in enumerate(K4_ORDER):
                    half, m = n // 2 % 2, n % 2
                    if m == 0:
                        dve.wait_ge(unit_done, c.next(unit_done))
                    signal = sum_signal(prepare, unit_taken if m else dve_step)
                    V.tensor_tensor(x[:, d, :], x[:, d, :], ps[:, 2 * half + m, :], ALU.add).then_inc(signal, c.made(signal))
                    if prepare:
                        finish_tile(d, K4_ORDER[n - 1] if n else None, n == KT - 1, prepare, m == 1)
                    if m:
                        c.unit.n += 1
                        if between:
                            between(n // 2)

            def scaled(dst, name=unit_taken, scale=None):
                dve.wait_ge(unit_done, c.next(unit_done))
                if scale is None:
                    i = V.tensor_tensor(dst, bank(), r_bc[:, :], ALU.mult)
                else:
                    i = V.scalar_tensor_tensor(dst, bank(), scale, r_bc[:, :], ALU.mult, ALU.mult)
                i.then_inc(name, c.made(name))
                c.unit.n += 1

            def hid_lo(k, src):
                dve.wait_ge(hi_made, c.next(hi_made))
                V.tensor_tensor(hl[:, k, :], src, hh[:, k, :].bitcast(F32), ALU.subtract).then_inc(hid_ready, c.made(hid_ready))

            dve.wait_ge(ext_landed, 16)
            V.tensor_copy(ext[:, 0:255], ext[:, 255:256].to_broadcast([ATT_HEADS, 255])).then_inc(dve_step, c.made(dve_step))
            V.memset(ext[:, 575:640], 0.0).then_inc(ext_built, c.made(ext_built))
            dve.wait_ge(turned, c.next(turned))
            for t, n in enumerate(FILLED):
                V.tensor_copy(prm[:, P * t:P * t + n], ps[:, 0, P * t:P * t + n]).then_inc(prm_ready, c.made(prm_ready))
            for d in range(KT):
                dve.wait_ge(turned, c.next(turned))
                V.tensor_copy(x[:, d, :], ps[:, (d + 1) % 8, :]).then_inc(x_added, c.made(x_added))
                finish_tile(d, d - 1 if d else None, d == KT - 1, ("norm", "norm_mix_g", 0), False)
            V.memset(upad[:, :, 0:PADC], 0.0).then_inc(dve_step, c.made(dve_step))
            V.memset(upad[:, :, PADC + SEQ:UPW], 0.0).then_inc(dve_step, c.made(dve_step))
            V.memset(apad[:, :, 0:1], 0.0).then_inc(dve_step, c.made(dve_step))
            V.memset(apad[:, :, SEQ + 1:SEQ + 2], 0.0).then_inc(dve_step, c.made(dve_step))

            for f in phases:
                nxt = next_prep(f)
                if f == "mix":
                    factor()
                    dve.wait_ge(ext_stored, 16)

                    conv_at = [0] * 4

                    def conv(pair, taps):
                        for _ in range(taps):
                            for t in (2 * pair, 2 * pair + 1):
                                k = conv_at[t]
                                if k == TAPS:
                                    continue
                                conv_at[t] += 1
                                dve.wait_ge(dve_step, c.of[dve_step].n - (1 if k else 0))
                                src, w = upad[:, t, k:k + SEQ], prow("conv_b_w", 4 * k + t)
                                if k == 0:
                                    i = V.tensor_scalar(cacc[:, t, :], src, w, prow("conv_b_b", t), ALU.mult, ALU.add)
                                else:
                                    i = V.scalar_tensor_tensor(cacc[:, t, :], src, w, cacc[:, t, :], ALU.mult, ALU.add)
                                i.then_inc(dve_step, c.made(dve_step))

                    def conv_step():
                        if conv_at[1] < TAPS:
                            conv(0, 4)
                        elif c.unit.n >= 8:
                            conv(1, 4)

                    for j in range(2):
                        for t in range(2):
                            scaled(upad[:, 2 * j + t, PADC:PADC + SEQ])
                            if j:
                                conv_step()
                        for t in range(2):
                            scaled(gbuf[:, t, :])
                        for t in range(2):
                            dve.wait_ge(curve_made, c.next(curve_made))
                            u = upad[:, 2 * j + t, PADC:PADC + SEQ]
                            V.tensor_tensor(u, u, gbuf[:, t, :], ALU.mult).then_inc(dve_step, c.made(dve_step))
                            dve.wait_ge(dve_step, c.now(dve_step))
                        if j:
                            conv_step()
                    for t in range(4):
                        scaled(apad[:, t, 1:1 + SEQ])
                        conv_step()
                    for t in range(4):
                        scaled(gbuf[:, t % 2, :])
                        dve.wait_ge(*c.own())
                        a = apad[:, t, 1:1 + SEQ]
                        V.tensor_tensor(a, a, gbuf[:, t % 2, :], ALU.mult).then_inc(dve_step, c.made(dve_step))
                        dve.wait_ge(dve_step, c.now(dve_step))
                        conv_step()
                    for t in range(4):
                        y = ybuf[:, t % 2, :]
                        if t >= 1:
                            hid_lo(t - 1, ybuf[:, (t - 1) % 2, :])
                        scaled(gbuf[:, t % 2, :])
                        V.tensor_scalar(y, apad[:, t, 0:SEQ], prow("conv_a_w", t), None, ALU.mult).then_inc(dve_step, c.made(dve_step))
                        dve.wait_ge(dve_step, c.now(dve_step))
                        for k in (1, 2):
                            V.scalar_tensor_tensor(y, apad[:, t, k:k + SEQ], prow("conv_a_w", 4 * k + t), y,
                                                           ALU.mult, ALU.add).then_inc(dve_step, c.made(dve_step))
                            dve.wait_ge(dve_step, c.now(dve_step))
                        V.tensor_tensor(y, y, gbuf[:, t % 2, :], ALU.mult).then_inc(to_hi, c.made(to_hi))
                        dve.wait_ge(to_hi, c.now(to_hi))
                        conv_step()
                    hid_lo(3, ybuf[:, 1, :])
                    while conv_at[3] < TAPS:
                        conv_step()
                    dve.wait_ge(*c.own())

                    def total(src):
                        V.tensor_tensor(ssq[:, :], src[0], src[1], ALU.add).then_inc(dve_step, c.made(dve_step))
                        dve.wait_ge(dve_step, c.now(dve_step))
                        V.tensor_tensor(ssq[:, :], ssq[:, :], src[2], ALU.add).then_inc(dve_step, c.made(dve_step))
                        dve.wait_ge(dve_step, c.now(dve_step))
                        V.tensor_tensor(ssq[:, :], ssq[:, :], src[3], ALU.add).then_inc(stats_in, c.made(stats_in))

                    tiles = [cacc[:, t, :] for t in range(4)]
                    squares = [apad[:, t, 0:SEQ] for t in range(4)]
                    total(tiles)

                    def layer_norm(n):
                        if n == 0:
                            dve.wait_ge(stats_done, c.next(stats_done))
                            V.tensor_scalar(t4, ps[:, 4, 0:ST], 1.0 / D_A, None, ALU.mult).then_inc(dve_step, c.made(dve_step))
                            dve.wait_ge(dve_step, c.now(dve_step))
                            diagonals(t4)
                        if n == 1:
                            for t in tiles:
                                V.tensor_tensor(t, t, ps[:, 5, :], ALU.subtract).then_inc(dve_step, c.made(dve_step))
                            dve.wait_ge(*c.own())
                            for t, s in zip(tiles, squares):
                                V.tensor_tensor(s, t, t, ALU.mult).then_inc(dve_step, c.made(dve_step))
                            dve.wait_ge(*c.own())
                            total(squares)
                        if n == 2:
                            dve.wait_ge(stats_done, c.next(stats_done))
                            mean_square(D_A, LN_EPS)
                            refine()
                            diagonals(rc)
                        if n == 3:
                            for t in tiles:
                                V.tensor_tensor(t, t, ps[:, 5, :], ALU.mult).then_inc(to_curve, c.made(to_curve))
                            for t in range(4):
                                hid_lo(4 + t, tiles[t])

                    out_units4(between=layer_norm)
                    out_units4(nxt)
                if f == "ffn":
                    V.memset(gpad[:, :, 0:1], 0.0).then_inc(dve_step, c.made(dve_step))
                    V.memset(gpad[:, :, SEQ + 1:SEQ + 2], 0.0).then_inc(dve_step, c.made(dve_step))

                    def chunk(i, tiles=8, prepare=None):
                        for b in range(tiles // 2):
                            for t in range(2):
                                w = [prow("conv_ffn_w", (FF // P) * k + 8 * i + 2 * b + t) for k in range(3)]
                                scaled(gpad[:, t, 1:1 + SEQ])
                                dve.wait_ge(*c.own())
                                g = gconv[:, t, :]
                                V.tensor_scalar(g, gpad[:, t, 0:SEQ], w[0], None, ALU.mult).then_inc(dve_step, c.made(dve_step))
                                dve.wait_ge(dve_step, c.now(dve_step))
                                V.scalar_tensor_tensor(g, gpad[:, t, 1:1 + SEQ], w[1], g, ALU.mult, ALU.add).then_inc(dve_step, c.made(dve_step))
                                dve.wait_ge(dve_step, c.now(dve_step))
                                V.scalar_tensor_tensor(g, gpad[:, t, 2:2 + SEQ], w[2], g, ALU.mult, ALU.add).then_inc(to_curve, c.made(to_curve))
                                if b and not t:
                                    hid_lo(2 * b - 1, hval[:, 1, :])
                            for t in range(2):
                                scaled(hval[:, t, :])
                                dve.wait_ge(*c.own())
                                dve.wait_ge(curve_made, c.next(curve_made))
                                V.tensor_tensor(hval[:, t, :], hval[:, t, :], gact[:, t, :], ALU.mult).then_inc(to_hi, c.made(to_hi))
                                if t:
                                    hid_lo(2 * b, hval[:, 0, :])
                        hid_lo(tiles - 1, hval[:, 1, :])
                        out_units8(prepare)
                    factor()
                    chunk(0)
                    chunk(1)
                    chunk(2, 6, nxt)
                if f == "ret":
                    dve.wait_ge(stats_done, c.next(stats_done))
                    V.tensor_scalar(ms2, ps[:, 4, ST:2 * ST], 1.0 / D, None, ALU.mult).then_inc(dve_step, c.made(dve_step))
                    mean_square(D, EPS)
                    refine()
                    V.tensor_copy(r1c, rc).then_inc(dve_step, c.made(dve_step))
                    dve.wait_ge(dve_step, c.now(dve_step))
                    V.tensor_tensor(t4, rc, rc, ALU.mult).then_inc(dve_step, c.made(dve_step))
                    dve.wait_ge(dve_step, c.now(dve_step))
                    V.tensor_tensor(t4, t4, ms2, ALU.mult).then_inc(dve_step, c.made(dve_step))
                    dve.wait_ge(dve_step, c.now(dve_step))
                    V.tensor_scalar(ms, t4, EPS, None, ALU.add).then_inc(to_curve, c.made(to_curve))
                    refine()
                    V.tensor_tensor(rc, rc, r1c, ALU.mult).then_inc(dve_step, c.made(dve_step))
                    dve.wait_ge(dve_step, c.now(dve_step))
                    diagonals(rc)
                    V.tensor_copy(r_bc[:, :], ps[:, 5, :]).then_inc(dve_step, c.made(dve_step))
                    dve.wait_ge(dve_step, c.now(dve_step))
                    diagonals(r1c)
                    V.tensor_copy(ssq[:, :], ps[:, 5, :]).then_inc(dve_step, c.made(dve_step))
                    dve.wait_ge(dve_step, c.now(dve_step))
                    dve.wait_ge(tab_landed, 48)
                    for t in (cos, sin):
                        V.tensor_tensor(t, t, r_bc[:, :], ALU.mult).then_inc(dve_step, c.made(dve_step))
                    dve.wait_ge(*c.own())

                    def rope(hi, lo):
                        dve.wait_ge(unit_done, c.next(unit_done))
                        dve.wait_ge(unit_done, c.next(unit_done))
                        a, b = ps[:, c.unit.n % 4, :], ps[:, (c.unit.n + 1) % 4, :]
                        V.tensor_tensor(sg[:, 0, :], a, cos, ALU.mult).then_inc(dve_step, c.made(dve_step))
                        V.tensor_tensor(sg[:, 1, :], a, sin, ALU.mult).then_inc(dve_step, c.made(dve_step))
                        V.tensor_tensor(sg[:, 2, :], b, sin, ALU.mult).then_inc(dve_step, c.made(dve_step))
                        V.tensor_tensor(sg[:, 3, :], b, cos, ALU.mult).then_inc(dve_step, c.made(dve_step))
                        dve.wait_ge(dve_step, c.now(dve_step))
                        V.tensor_tensor(sg[:, 0, :], sg[:, 0, :], sg[:, 2, :], ALU.subtract).then_inc(unit_taken, c.made(unit_taken, 2))
                        V.tensor_tensor(sg[:, 1, :], sg[:, 1, :], sg[:, 3, :], ALU.add).then_inc(to_hi, c.made(to_hi))
                        c.unit.n += 1
                        c.unit.n += 1
                        dve.wait_ge(hi_made, c.next(hi_made))
                        dve.wait_ge(*c.own())
                        V.tensor_tensor(lo[:, :, :], sg[:, 0:2, :], hi[:, :, :].bitcast(F32), ALU.subtract).then_inc(qk_ready, c.made(qk_ready))
                        dve.wait_ge(*c.own())

                    def score_lo(j):
                        cut = slice(BY_KEY[j], BY_KEY[j] + SEQ - P * j)
                        dve.wait_ge(hi_made, c.next(hi_made))
                        V.tensor_tensor(ptl[:, cut], ptf[:, cut], pth[:, cut].bitcast(F32), ALU.subtract).then_inc(
                            pt_ready, c.made(pt_ready))

                    def head(h, prepare=None, first=False):
                        rope(qh, ql)
                        rope(kh, kl)

                        def v_unit(n):
                            value_lo(hh[:, 4:8, :], hl[:, 4:8, :], 256 * (n // 2))
                        for n in range(3):
                            v_unit(n)
                        for j in range(ST):
                            dve.wait_ge(scores_done, c.next(scores_done))
                            n = SEQ - P * j
                            cut = slice(BY_KEY[j], BY_KEY[j] + n)
                            dec = decay[:, h, 0:n] if isinstance(h, int) else \
                                decay[:, bass.ds(h, 1), 0:n].rearrange("p a b -> p (a b)")
                            V.tensor_tensor(ptf[:, cut], ps[:, 4 + j, 0:n], dec, ALU.mult).then_inc(to_hi, c.made(to_hi))
                            if j:
                                score_lo(j - 1)
                        score_lo(ST - 1)
                        v_unit(3)
                        scaled(sg[:, 0, :])
                        if first:
                            for d in range(KT):
                                V.tensor_tensor(x[:, d, :], x[:, d, :], ssq[:, :], ALU.mult).then_inc(dve_step, c.made(dve_step))
                        c.next(curve_made)
                        for i in range(ST):
                            dve.wait_ge(curve_made, c.next(curve_made))
                            V.bn_stats(bn, o_sb[:, i, :]).then_inc(dve_step, c.made(dve_step))
                            dve.wait_ge(dve_step, c.now(dve_step))
                            V.bn_aggr(mv[:, i, :], bn).then_inc(o_taken, c.made(o_taken))
                            dve.wait_ge(o_taken, c.now(o_taken))
                        V.tensor_scalar(ms, mv[:, :, 1], EPS, None, ALU.add).then_inc(to_curve, c.made(to_curve))
                        refine_root()
                        for i in range(ST):
                            V.tensor_scalar(o_sb[:, i, :], o_sb[:, i, :], mv[:, i, 0:1], rc2[:, i:i + 1],
                                                 ALU.subtract, ALU.mult).then_inc(p_ready, c.made(p_ready))
                        scaled(sg[:, 1, :])
                        scaled(sg[:, 2, :])

                        def gated(j):
                            dve.wait_ge(turned, c.next(turned))
                            if j:
                                dve.wait_ge(curve_made, c.next(curve_made))
                            g = prow("ret_gn_g_2", 4 * h + j)
                            V.scalar_tensor_tensor(sg[:, j, :], ps[:, 4 + j, :], g, sg[:, j, :], ALU.mult, ALU.mult).then_inc(to_hi, c.made(to_hi))

                        for j in range(3):
                            gated(j)
                            if j:
                                hid_lo(j - 1, sg[:, j - 1, :])
                        scaled(sg[:, 3, :])
                        hid_lo(2, sg[:, 2, :])
                        gated(3)
                        hid_lo(3, sg[:, 3, :])
                        out_units4(prepare)

                    rc2 = t4

                    def refine_root():
                        dve.wait_ge(curve_made, c.next(curve_made))
                        V.reciprocal(rc2, root).then_inc(dve_step, c.made(dve_step))
                        dve.wait_ge(dve_step, c.now(dve_step))
                        V.tensor_tensor(ms2, rc2, rc2, ALU.mult).then_inc(dve_step, c.made(dve_step))
                        dve.wait_ge(dve_step, c.now(dve_step))
                        V.tensor_tensor(ms2, ms2, ms, ALU.mult).then_inc(dve_step, c.made(dve_step))
                        dve.wait_ge(dve_step, c.now(dve_step))
                        V.tensor_scalar(ms2, ms2, -0.5, 1.5, ALU.mult, ALU.add).then_inc(dve_step, c.made(dve_step))
                        dve.wait_ge(dve_step, c.now(dve_step))
                        V.tensor_tensor(rc2, rc2, ms2, ALU.mult).then_inc(dve_step, c.made(dve_step))
                        dve.wait_ge(dve_step, c.now(dve_step))

                    def value_lo(hi, lo, c0):
                        dve.wait_ge(unit_done, c.next(unit_done))
                        dve.wait_ge(hi_made, c.next(hi_made))
                        half = c.unit.n % 2
                        for m in range(2):
                            s = 2 * half + m
                            signal = unit_taken if m else dve_step
                            V.scalar_tensor_tensor(lo[:, s, c0:c0 + 256], bank()[:, 256 * m:256 * (m + 1)], rc[:, s:s + 1],
                                                        hi[:, s, c0:c0 + 256].bitcast(F32), ALU.mult, ALU.subtract).then_inc(signal, c.made(signal))
                        c.unit.n += 1

                    head(0, first=True)
                    head(1)
                    head(2)
                    head(3, nxt)
                if f in ("mlp0", "mlp1"):
                    if f == "mlp0" and "att" in phases:
                        V.memset(bias[0:64, :, 448:512], MASKED).then_inc(dve_step, c.made(dve_step))
                    def chunk(i, prepare=None):
                        for u in range(8):
                            dve.wait_ge(unit_done, c.next(unit_done))
                            h = hval[:, u % 2, :]
                            dve.wait_ge(*c.own())
                            V.scalar_tensor_tensor(h, bank(), 0.0, r_bc[:, :], ALU.max, ALU.mult).then_inc(unit_taken, c.made(unit_taken))
                            dve.wait_ge(unit_taken, c.now(unit_taken))
                            c.unit.n += 1
                            V.tensor_tensor(h, h, h, ALU.mult).then_inc(to_hi, c.made(to_hi))
                            if u:
                                hid_lo(u - 1, hval[:, (u - 1) % 2, :])
                        hid_lo(KT - 1, hval[:, 1, :])
                        out_units8(prepare)
                    factor()
                    c.repeat(MLP_CHUNKS - 1, chunk)
                    chunk(MLP_CHUNKS - 1, nxt)
                if f == "att":
                    banks[0] = 2
                    factor()

                    def value_lo():
                        dve.wait_ge(unit_done, c.next(unit_done))
                        dve.wait_ge(hi_made, c.next(hi_made))
                        half = c.unit.n % 2
                        for m in range(2):
                            s = 2 * half + m
                            signal = unit_taken if m else dve_step
                            V.scalar_tensor_tensor(avl[:, s, :], bank()[:, 256 * m:256 * (m + 1)], rc[:, s:s + 1],
                                                        avh[:, s, :].bitcast(F32), ALU.mult, ALU.subtract).then_inc(signal, c.made(signal))
                        c.unit.n += 1

                    def qk_unit(n):
                        hi, lo = ((qh, ql), (kh, kl))[n % 2]
                        scaled(hval[:, n % 2, :], scale=0.125 if n % 2 == 0 else 1.0)
                        dve.wait_ge(hi_made, c.next(hi_made))
                        dve.wait_ge(*c.own())
                        V.tensor_tensor(lo[:, n // 2, :], hval[:, n % 2, :], hi[:, n // 2, :].bitcast(F32), ALU.subtract).then_inc(qk_ready, c.made(qk_ready))

                    def maxima(h):
                        dve.wait_ge(bias_landed[h % 4], 32 * (h // 4 + 1))
                        for i, (bk, at) in SCORES.items():
                            n = P * (i + 1)
                            if i != 2:
                                dve.wait_ge(scores_done, c.next(scores_done))
                            V.tensor_tensor_reduce(probs[:, h % 2, BY_QUERY[i]:BY_QUERY[i] + n], ps[:, bk, at:at + n],
                                                        bias[:, h % 4, SEQ - n:SEQ], 1.0, MASKED, ALU.add, ALU.max,
                                                        mx[:, i:i + 1]).then_inc(s_taken, c.made(s_taken))
                        dve.wait_ge(*c.own())
                        V.tensor_scalar(nmx, mx, -1.0, None, ALU.mult).then_inc(to_curve, c.made(to_curve))

                    def normalise(h):
                        dve.wait_ge(curve_made, c.next(curve_made))
                        V.reciprocal(rinv, rs).then_inc(dve_step, c.made(dve_step))
                        dve.wait_ge(dve_step, c.now(dve_step))
                        for i in range(ST):
                            cut = slice(BY_QUERY[i], BY_QUERY[i] + P * (i + 1))
                            signal = p_ready if i == ST - 1 else dve_step
                            V.tensor_scalar(probs[:, h % 2, cut], probs[:, h % 2, cut], rinv[:, i:i + 1], None, ALU.mult).then_inc(signal, c.made(signal))

                    def probs_lo():
                        for bk, at, n in TURNED:
                            dve.wait_ge(hi_made, c.next(hi_made))
                            cut = slice(at, at + n)
                            V.tensor_tensor(ptl[:, cut], ps[:, bk, 0:n], pth[:, cut].bitcast(F32), ALU.subtract).then_inc(pt_ready, c.made(pt_ready))

                    def mixed_lo(h):
                        rows = slice(64 * (h % 2), 64 * (h % 2) + 64)
                        dve.wait_ge(hi_made, c.next(hi_made))
                        V.tensor_tensor(hl[rows, h // 2, :], ps[rows, 7, :], hh[rows, h // 2, :].bitcast(F32),
                                             ALU.subtract).then_inc(hid_ready, c.made(hid_ready))

                    for n in range(4):
                        qk_unit(n)
                    maxima(0)
                    normalise(0)
                    for h in range(ATT_HEADS):
                        s, more = h % 4, h < ATT_HEADS - 4
                        if h + 1 < ATT_HEADS:
                            maxima(h + 1)
                        if s == 0:
                            if h:
                                mixed_lo(h - 1)
                            value_lo()
                            probs_lo()
                            if h + 1 < ATT_HEADS:
                                normalise(h + 1)
                            value_lo()
                            continue
                        if more:
                            qk_unit((0, 0, 2, 3)[s])
                        mixed_lo(h - 1)
                        probs_lo()
                        if h + 1 < ATT_HEADS:
                            normalise(h + 1)
                        if s == 1 and more:
                            qk_unit(1)
                    mixed_lo(ATT_HEADS - 1)
                    banks[0] = 4
                    out_units8(nxt)
            dve.wait_ge(stats_done, c.next(stats_done))
            mean_square(D, EPS)
            refine(rc_final)
            for i in range(ST):
                dve.wait_ge(turned, turned_total + 2 * i + 2)
                V.tensor_scalar(work[:, i * D + 512:(i + 1) * D], ps[:, (1, 3, 6, 4)[i], :], rc[:, i:i + 1], None,
                                ALU.mult).then_inc(out_ready_dve, 1)


PHASES = ["mix", "ffn", "ret", "mlp0", "att", "mlp1"]
_INS = ["x", "norm_mix_g", "w_in", "conv_a_w", "conv_b_w", "conv_b_b", "ln_b_g", "ln_b_b", "w_out", "norm_ffn_g",
        "w_gate", "w_up", "conv_ffn_w", "w_down", "norm_final_g", "mix_norm_g_2", "ret_w_in_2", "ret_gn_g_2",
        "ret_w_out_2", "att_w_in_2", "att_rel_bias_2", "att_w_out_2", "mlp_norm_g_2", "mlp_w1_2", "mlp_w2_2",
        "final_norm_g_2"]


def constants():
    half = D // RET_HEADS // 2
    f = np.float32
    inv = np.exp(-np.log(f(10000.0)) * np.arange(half, dtype=f) / f(half)).astype(f)
    angle = (inv[:, None] * np.arange(SEQ, dtype=f)[None, :]).astype(f).astype(np.float64)
    log_gamma = np.log1p(-np.exp2(-5.0 - np.arange(RET_HEADS)))
    key, query = np.arange(P)[:, None], np.arange(SEQ)[None, :]
    decay = np.exp(log_gamma[:, None, None] * np.abs(query - key)) * (query // 64 >= key // 64)
    decay = decay * (D // RET_HEADS) ** -0.5
    return {"ident": np.eye(P, dtype=f), "cos": np.cos(angle).astype(f), "sin": np.sin(angle).astype(f),
            "decay": np.ascontiguousarray(decay.transpose(1, 0, 2)).astype(f)}


def program(nc, a, phases=PHASES):
    stacked = []
    for name, (at, n) in ROWS.items():
        v = a[name]
        dims = " ".join("abc"[:len(v.shape) - 1])
        v = v.rearrange(f"{dims} (t p) -> ({dims} t) p", p=P)
        stacked.append((v, (at, at + n)))
    consts = [a["const_ident"], a["const_cos"], a["const_sin"], a["const_decay"]]
    build(nc, phases, a["x"][0], a["w_in"][0], a["w_out"][0], a["w_gate"][0], a["w_up"][0], a["w_down"][0],
          a["ret_w_in_2"][0], a["ret_w_out_2"][0], a["att_w_in_2"][0], a["att_w_out_2"][0],
          [a["mlp_w1_2"][m] for m in range(2)], [a["mlp_w2_2"][m] for m in range(2)], a["att_rel_bias_2"][0],
          stacked, consts, a["out"][0])


def kernel(**inputs):
    import concourse.bacc as _bacc
    from concourse.bass_utils import run_bass_kernel_spmd as _run

    nc = _bacc.Bacc("TRN2", target_bir_lowering=False, num_devices=1)
    arrays, tensors = {}, {}
    given = {name: np.ascontiguousarray(inputs[name]) for name in _INS}
    given.update({f"const_{name}": v for name, v in constants().items()})
    for name, v in given.items():
        arrays[f"in_{name}_dram"] = v
        tensors[name] = nc.dram_tensor(f"in_{name}_dram", v.shape, mybir.dt.from_np(v.dtype), kind="ExternalInput").ap()
    tensors["out"] = nc.dram_tensor("out_0_dram", (1, SEQ, D), F32, kind="ExternalOutput").ap()
    program(nc, tensors)
    r = _run(nc, [arrays], core_ids=[0])
    return r.results[0]["out_0_dram"]
```

```python
from contextlib import ExitStack

import concourse.bass as bass
from concourse import mybir
import numpy as np

F32 = mybir.dt.float32
F32R = mybir.dt.float32r
ALU = mybir.AluOpType
ACT = mybir.ActivationFunctionType

P = 128
SEQ = 512
D = 1024
KT = D // P
ST = SEQ // P
HALF = 128
FF = 2816
D_A = 512
TAPS = 31
PADC = TAPS // 2
UPW = SEQ + 2 * PADC
RET_HEADS = 4
ATT_HEADS = 16
MLP_CHUNKS = 4
EPS = 1e-6
LN_EPS = 1e-5
REL = 320
MASKED = -3.0e38

MIX_UNITS = 20
ROWS = {}
_at = 0
for _name, _n in (("norm_mix_g", 8), ("conv_a_w", 12), ("conv_b_b", 4), ("ln_b_g", 4), ("ln_b_b", 4),
                  ("norm_ffn_g", 8), ("norm_final_g", 8), ("mix_norm_g_2", 16), ("ret_gn_g_2", 16),
                  ("mlp_norm_g_2", 16), ("final_norm_g_2", 8), ("conv_b_w", 124), ("conv_ffn_w", 66)):
    ROWS[_name] = (_at, _n)
    _at += _n
N_ROWS = _at
TENSOR_TAPS = 11
FIRST_TAP_UNIT = MIX_UNITS - TENSOR_TAPS
FIRST_TAP = [0, 0, TENSOR_TAPS, TENSOR_TAPS]
POOL_SQUARES = (5, 6, 7)
X_LOADS = 4

BY_KEY = [0, 640, 1024, 512]
BY_QUERY = [0, 1024, 128, 512]
PACKED = 1280
TURNED = ((4, 0, 512), (5, 512, 512), (6, 1024, 256))
SCORES = {0: (2, 0), 2: (2, 128), 3: (3, 0), 1: (2, 0)}

K4_ORDER = [0, 2, 1, 3, 4, 6, 5, 7]
NATURAL = list(range(KT))


class Count:

    def __init__(self):
        self.n, self.turn, self.per = 0, None, 0

    def value(self, off=0):
        return self.n + off if self.turn is None else self.turn * self.per + (self.n + off)

    def beyond(self, k):
        return self.turn is not None or self.n > k


class Counts:

    def __init__(self, engine, sems):
        self.engine = engine
        self.of = {s: Count() for s in sems}
        self.block, self.unit = Count(), Count()
        self.latest = None

    def made(self, sem, k=1):
        self.of[sem].n += k
        self.latest = sem
        return k

    def next(self, sem, k=1):
        self.of[sem].n += k
        return self.of[sem].value()

    def now(self, sem):
        return self.of[sem].value()

    def own(self):
        return self.latest, self.of[self.latest].value()

    def repeat(self, turns, body):
        every = [*self.of.values(), self.block, self.unit]
        before = [x.n for x in every]
        body(0)
        per = [x.n - b for x, b in zip(every, before)]
        if turns == 1:
            return
        with self.engine.Fori(1, turns) as i:
            for x, b, p in zip(every, before, per):
                x.n, x.per, x.turn = b, p, i
            body(i)
        for x, b, p in zip(every, before, per):
            assert x.n - b == p
            x.n, x.turn = b + turns * p, None


def build(nc, phases, x_in, w_in, w_out, w_gate, w_up, w_down, ret_w_in, ret_w_out, att_w_in,
          att_w_out, w1, w2, rel_bias, params, consts, out):
    ident_c, cos_c, sin_c, decay_c = consts
    x_tiles = x_in.rearrange("(k p) s -> p k s", p=P)
    ctx = ExitStack()
    with ctx:
        def sb(name, shape, dt=F32):
            return ctx.enter_context(nc.sbuf_tensor(name, shape, dt))

        x = sb("x", [P, KT, SEQ])
        xh = sb("xh", [P, KT, SEQ], F32R)
        xl = sb("xl", [P, KT, SEQ], F32R)
        hh = sb("hid_hi", [P, KT, SEQ], F32R)
        hl = sb("hid_lo", [P, KT, SEQ], F32R)
        raw = sb("raw", [P, 2, 2048])
        wh = sb("w_hi", [P, 2, 2048], F32R)
        wl = sb("w_lo", [P, 2, 2048], F32R)
        qh = sb("q_hi", [P, 2, SEQ], F32R)
        ql = sb("q_lo", [P, 2, SEQ], F32R)
        kh = sb("k_hi", [P, 2, SEQ], F32R)
        kl = sb("k_lo", [P, 2, SEQ], F32R)
        avh = sb("att_v_hi", [P, ST, 256], F32R)
        avl = sb("att_v_lo", [P, ST, 256], F32R)
        pth = sb("probs_t_hi", [P, PACKED], F32R)
        ptl = sb("probs_t_lo", [P, PACKED], F32R)
        work = sb("work", [P, 8448])
        r_bc = sb("r_bc", [P, SEQ])
        ssq = sb("sum_of_squares", [P, SEQ])
        diag_rows = sb("diagonals", [P, SEQ])
        ident = sb("ident", [P, P])
        ones = sb("ones", [P, P])
        prm = sb("prm", [P, N_ROWS])
        cols = sb("cols", [P, 64])
        tap_w = sb("tap_w", [P, 4, 2, P])
        ps = ctx.enter_context(nc.psum_tensor("ps", [P, 8, SEQ], F32))
        bias_dram = nc.dram_tensor("bias_by_query", (ATT_HEADS, P, SEQ), F32).ap()

        diag = diag_rows[:, :].rearrange("p (i c) -> p i c", i=ST)
        ms, root, rc, t4 = (cols[:, 4 * k:4 * k + 4] for k in range(4))
        ms2, r1c = cols[:, 16:20], cols[:, 20:24]
        mv = cols[:, 24:32].rearrange("p (i c) -> p i c", c=2)
        mx, nmx, rs, rinv = (cols[:, 32 + 4 * k:36 + 4 * k] for k in range(4))
        bn = cols[:, 48:54]

        def part(at, *shape):
            n = int(np.prod(shape))
            v = work[:, at:at + n]
            return v if len(shape) == 1 else v.rearrange("p (a b) -> p a b", a=shape[0])

        upad, cacc, apad, gbuf, ybuf = (part(0, 4, UPW), part(2168, 4, SEQ), part(4216, 4, SEQ + 2),
                                        part(6272, 2, SEQ), part(7296, 2, SEQ))
        ln_squares = [apad[:, t, 0:SEQ] for t in range(4)]
        x_squares, ext = part(0, KT, SEQ), work[0:ATT_HEADS, 7296:7936]
        gpad, gconv, gact, hval = part(3072, 2, SEQ + 2), part(4100, 2, SEQ), part(5124, 2, SEQ), part(6148, 2, SEQ)
        cos, sin, decay = part(0, SEQ), part(512, SEQ), part(1024, RET_HEADS, SEQ)
        sg, o_sb, ptf = part(3072, 4, SEQ), part(5120, ST, SEQ), part(7168, PACKED)
        squares = part(5124, 4, SEQ)
        bias, probs = part(0, 4, SEQ), part(2048, 2, PACKED)

        def prow(name, r):
            at, n = ROWS[name]
            assert r < n if isinstance(r, int) else True
            if isinstance(r, int):
                return prm[:, at + r:at + r + 1]
            return prm[:, bass.ds(r + at, 1)]

        sems = []

        def sem(name):
            sems.append(ctx.enter_context(nc.semaphore(name)))
            return sems[-1]

        w_landed = [sem(f"w_landed{i}") for i in range(2)]
        bias_landed = [sem(f"bias_landed{i}") for i in range(4)]
        w_hi = sem("w_hi")
        w_lo = sem("w_lo")
        unit_done = sem("unit_done")
        unit_taken = sem("unit_taken")
        x_added = sem("x_added")
        x_ready = sem("x_ready")
        hid_ready = sem("hid_ready")
        hi_made = sem("hi_made")
        curve_made = sem("curve_made")
        to_hi = sem("to_hi")
        to_curve = sem("to_curve")
        stats_in = sem("stats_in")
        stats_done = sem("stats_done")
        turned = sem("turned")
        scores_done = sem("scores_done")
        mixed_done = sem("mixed_done")
        qk_ready = sem("qk_ready")
        pt_ready = sem("pt_ready")
        p_ready = sem("p_ready")
        s_taken = sem("s_taken")
        o_copied = sem("o_copied")
        dve_step = sem("dve_step")
        x_landed = [sem(f"x_landed{i}") for i in range(X_LOADS)]
        p_landed = sem("p_landed")
        c_landed = sem("c_landed")
        ext_landed = sem("ext_landed")
        ext_built = sem("ext_built")
        ext_stored = sem("ext_stored")
        tab_landed = sem("tab_landed")
        out_ready = sem("out_ready")
        out_stored = sem("out_stored")
        pool_squared = sem("pool_squared")
        ones_set = sem("ones_set")
        u_ready = sem("u_ready")
        taps_made = sem("taps_made")
        taps_done = sem("taps_done")
        conv_done = sem("conv_done")
        act_step = sem("act_step")

        turned_before_att = 4 * RET_HEADS if "ret" in phases else 0
        block = ctx.enter_context(nc.Block())

        n_blocks = sum({"mix": 14, "ffn": 34, "ret": 32, "mlp0": 32, "att": 16, "mlp1": 32}[f] for f in phases)

        def next_prep(f):
            k = phases.index(f) + 1
            if k == len(phases):
                return ("final", "final_norm_g_2", 0)
            return {"ffn": ("norm", "norm_ffn_g", 0), "ret": ("double", "mix_norm_g_2", 0),
                    "mlp0": ("norm", "mlp_norm_g_2", 0), "att": ("norm", "mix_norm_g_2", 8),
                    "mlp1": ("norm", "mlp_norm_g_2", 8)}[phases[k]]

        @block.sync
        def _(sp):
            c = Counts(sp, sems)

            def load(matrix, k0, nk, c0, width):
                slot = c.block.n % 2
                if c.block.beyond(1):
                    sp.wait_ge(w_lo, 2 * c.block.value(-1))
                dst = raw[:, slot, 0:nk * width].rearrange("p (k c) -> p k c", k=nk)
                rows = slice(k0, k0 + nk) if isinstance(k0, int) else bass.ds(k0, nk)
                wide = slice(c0, c0 + width) if isinstance(c0, int) else bass.ds(c0, width)
                src = matrix.rearrange("(k p) f -> p k f", p=P)[:, rows, wide]
                sp.dma_start(dst, src).then_inc(w_landed[slot], c.made(w_landed[slot], 16))
                c.block.n += 1

            def outs_k4(matrix, k0):
                for b in range(2):
                    load(matrix, k0, 4, 512 * b, 512)

            def outs_k8(matrix, k0, nk=KT):
                for b in range(4):
                    load(matrix, k0, nk, 256 * b, 256)

            for f in phases:
                if f == "mix":
                    for j in range(2):
                        load(w_in, 0, KT, 3 * D_A + 256 * j, 256)
                        if j == 0:
                            n = KT // X_LOADS
                            sp.dma_start(x[:, 0:n, :], x_tiles[:, 0:n, :]).then_inc(x_landed[0], 16)
                        load(w_in, 0, KT, 4 * D_A + 256 * j, 256)
                    for c0 in (0, 2 * D_A, D_A):
                        for j in range(2):
                            load(w_in, 0, KT, c0 + 256 * j, 256)
                    outs_k4(w_out, 0)
                    outs_k4(w_out, 4)
                if f == "ffn":
                    def chunk(i, tiles=8):
                        for b in range(tiles // 2):
                            load(w_gate, 0, KT, i * 1024 + 256 * b, 256)
                            load(w_up, 0, KT, i * 1024 + 256 * b, 256)
                        outs_k8(w_down, i * 8, tiles)
                    c.repeat(2, chunk)
                    chunk(2, 6)
                if f == "ret":
                    def head(h):
                        load(ret_w_in, 0, KT, h * 256, 256)
                        load(ret_w_in, 0, KT, h * 256 + 1024, 256)
                        for c0 in (2048, 2304, 4096, 4352):
                            load(ret_w_in, 0, KT, h * 512 + c0, 256)
                        outs_k4(ret_w_out, h * 4)
                    c.repeat(RET_HEADS, head)
                if f == "att":
                    def group(g):
                        for c0 in (0, 1024, 2048):
                            load(att_w_in, 0, KT, g * 256 + c0, 256)
                    def group_pair(gp):
                        group(gp * 2)
                        group(gp * 2 + 1)
                    c.repeat(2, group_pair)
                    outs_k4(att_w_out, 0)
                    outs_k4(att_w_out, 4)
                if f in ("mlp0", "mlp1"):
                    m = int(f[-1])
                    def chunk(i, m=m):
                        for b in range(4):
                            load(w1[m], 0, KT, i * 1024 + 256 * b, 256)
                        outs_k8(w2[m], i * 8)
                    c.repeat(MLP_CHUNKS, chunk)
            assert c.block.n == n_blocks
            for n in range(KT):
                sp.wait_ge(out_ready, n + 1)
                sp.dma_start(out[P * n:P * (n + 1), :], x[:, n, :]).then_inc(out_stored, 16)
            sp.wait_ge(out_stored, 16 * KT)

        @block.gpsimd
        def _(pool):
            c = Counts(pool, sems)
            nc.gpsimd.memset(ones[:, :], 1.0).then_inc(ones_set, 1)

            def pair(i, first=False):
                for slot in range(2):
                    for half in range(2):
                        if first and (slot, half) == (1, 0):
                            pool.wait_ge(x_landed[X_LOADS - 1], 16)
                            pool.wait_ge(x_landed[X_LOADS - 2], 16)
                            for d in POOL_SQUARES:
                                nc.gpsimd.tensor_tensor(x_squares[:, d, :], x[:, d, :], x[:, d, :], ALU.mult).then_inc(
                                    pool_squared, c.made(pool_squared))
                        pool.wait_ge(w_hi, c.next(w_hi))
                        cut = (slice(None), slot, slice(None), slice(HALF * half, HALF * (half + 1)))
                        view = [t[:, :, :].rearrange("p s (k c) -> p s k c", c=256)[cut] for t in (wl, raw, wh)]
                        nc.gpsimd.tensor_tensor(view[0], view[1], view[2].bitcast(F32), ALU.subtract).then_inc(w_lo, c.made(w_lo))
            pair(0, first=True)
            c.repeat(n_blocks // 2 - 1, pair)

        @block.tensor
        def _(pe):
            c = Counts(pe, sems)
            banks = [4]

            def product(o, a, b, first, last):
                nc.tensor.matmul(o, a[0], b[0], start=first, stop=False, skip_group_check=True)
                nc.tensor.matmul(o, a[0], b[1], start=False, stop=False, skip_group_check=True)
                return nc.tensor.matmul(o, a[1], b[0], start=False, stop=last, skip_group_check=True)

            def weights(slot, width):
                return [t[:, slot, :].rearrange("p (k c) -> p k c", c=width) for t in (wh, wl)]

            def unit8(rhs, nk=KT, fresh=None, slot=None, half=None, ahead=1, between=None):
                slot = c.unit.n // 2 % 2 if slot is None else slot
                half = c.unit.n % 2 if half is None else half
                pe.wait_ge(w_lo, c.unit.value(ahead))
                others = banks[0] - 1 if fresh is None else fresh
                if c.unit.beyond(others):
                    pe.wait_ge(unit_taken, c.unit.value(-others))
                w = weights(slot, 256)
                for k in range(nk):
                    if between and k == nk // 2:
                        between()
                    a = [t[:, k, HALF * half:HALF * (half + 1)] for t in w]
                    mm = product(ps[:, c.unit.n % banks[0], :], a, [t[:, k, :] for t in rhs], k == 0, k == nk - 1)
                mm.then_inc(unit_done, c.made(unit_done))
                c.unit.n += 1

            def unit4(rhs, k0, ready=None, fresh=False, bank0=None):
                slot, half = c.unit.n // 2 % 2, c.unit.n % 2
                pe.wait_ge(w_lo, c.unit.value(1))
                pe.wait_ge(unit_taken, c.unit.value(0 if fresh else -1))
                w = weights(slot, 512)
                for m, k in [(m, k) for tiles in ((0, 1, 2), (3,)) for m in range(2) for k in tiles]:
                    if ready and m == 0:
                        pe.wait_ge(ready, c.next(ready))
                    f = half + 2 * m
                    a = [t[:, k, P * f:P * (f + 1)] for t in w]
                    bank = (2 * half if bank0 is None else bank0) + m
                    mm = product(ps[:, bank, :], a, [t[:, k0 + k, :] for t in rhs], k == 0, k == 3)
                mm.then_inc(unit_done, c.made(unit_done))
                c.unit.n += 1

            def unit_v(lhs):
                slot, half = c.unit.n // 2 % 2, c.unit.n % 2
                pe.wait_ge(w_lo, c.unit.value(2 - half))
                pe.wait_ge(unit_taken, c.unit.value(1 - banks[0]))
                w = weights(slot, 256)
                for m in range(2):
                    s = 2 * half + m
                    for k in range(KT):
                        a = [t[:, k, P * s:P * (s + 1)] for t in lhs]
                        mm = product(ps[:, c.unit.n % banks[0], 256 * m:256 * (m + 1)], a, [t[:, k, :] for t in w],
                                     k == 0, k == KT - 1)
                mm.then_inc(unit_done, c.made(unit_done))
                c.unit.n += 1

            def column_sums(src, col=0):
                for i in range(ST):
                    mm = nc.tensor.matmul(ps[:, 4, col + i:col + i + 1], src[:, P * i:P * (i + 1)], ones[:, 0:1],
                                          start=True, stop=True, skip_group_check=True)
                return mm

            def stats(second=None):
                pe.wait_ge(stats_in, c.next(stats_in))
                mm = column_sums(ssq)
                if second is not None:
                    mm = column_sums(second, 4)
                mm.then_inc(stats_done, c.made(stats_done))

            def spread():
                pe.wait_ge(stats_in, c.next(stats_in))
                for i in range(ST):
                    mm = nc.tensor.matmul(ps[:, 5, P * i:P * (i + 1)], ones[:, :], diag[:, i, :],
                                          start=True, stop=True, skip_group_check=True)
                mm.then_inc(stats_done, c.made(stats_done))

            X, H = (xh, xl), (hh, hl)

            def unit_pair(rhs, nk=KT, order=None, ready=None, fresh=False, across=False, between=None):
                order = order or list(range(nk))
                late = nk // 2
                for part in (order[:-late], order[-late:]):
                    for n in range(2):
                        if between and n and part[0] != order[0]:
                            between()
                        first = part[0] == order[0]
                        if first:
                            pe.wait_ge(w_lo, c.unit.value(1 + (2 * n if across else n)))
                            others = 1 if fresh else banks[0] - 1 - n
                            if c.unit.beyond(others):
                                pe.wait_ge(unit_taken, c.unit.value(-others))
                        slot, half = (c.unit.n // 2 + n) % 2 if across else c.unit.n // 2 % 2, 0 if across else n
                        w = weights(slot, 256)
                        for k in part:
                            if n == 0:
                                pe.wait_ge(ready, c.next(ready))
                            a = [t[:, k, HALF * half:HALF * (half + 1)] for t in w]
                            mm = product(ps[:, (c.unit.n + n) % banks[0], :], a, [t[:, k, :] for t in rhs],
                                         k == order[0], k == order[-1])
                        if not first:
                            mm.then_inc(unit_done, c.made(unit_done))
                c.unit.n += 2

            def first_units(order, double=False):
                unit_pair(X, order=order, ready=x_ready, fresh=True, between=lambda: stats(r_bc if double else None))
                unit8(X, between=spread)
                unit8(X)

            order = NATURAL
            for f in phases:
                if f == "mix":
                    first_units(order)
                    for u in range(4, MIX_UNITS):
                        unit8(X)
                        g = u - FIRST_TAP_UNIT
                        if g < 0:
                            continue
                        if g == 0:
                            pe.wait_ge(u_ready, 1)
                        pe.wait_ge(taps_made, c.next(taps_made))
                        for m in range(2):
                            mm = nc.tensor.matmul(ps[:, 6 + m, :], tap_w[:, g % 4, m, :], upad[:, 2 + m, g:g + SEQ],
                                                  start=g == 0, stop=g == TENSOR_TAPS - 1, skip_group_check=True)
                    mm.then_inc(taps_done, c.made(taps_done))
                    unit4(H, 0, ready=hid_ready, fresh=True)
                    for t in range(4):
                        pe.wait_ge(conv_done, c.next(conv_done))
                        mm = nc.tensor.matmul(ps[:, 5, :], ones[:, :], cacc[:, t, :], start=t == 0, stop=t == 3,
                                              skip_group_check=True)
                    mm.then_inc(stats_done, c.made(stats_done))
                    unit4(H, 0)
                    stats()
                    unit4(H, 0)
                    spread()
                    unit4(H, 0)
                    unit4(H, 4, ready=hid_ready)
                    for _ in range(3):
                        unit4(H, 4)
                    order = K4_ORDER
                if f == "ffn":
                    def chunk(i, tiles=8, first=False):
                        if first:
                            first_units(order)
                        for _ in range(4 if first else 0, 2 * tiles):
                            unit8(X)
                        unit_pair(H, tiles, ready=hid_ready)
                        for _ in range(6):
                            unit8(H, tiles)
                    chunk(0, first=True)
                    chunk(1)
                    chunk(2, 6)
                    order = NATURAL
                if f == "ret":
                    def head(h, first=False):
                        if first:
                            first_units(order, double=True)
                        else:
                            for n in range(4):
                                unit8(X, fresh=(1, 2, 2, 3)[n])
                        for n in range(3):
                            unit_v(X)
                            if first and n == 0:
                                spread()
                        pe.wait_ge(qk_ready, c.next(qk_ready, 2))
                        for j in range(ST):
                            n = SEQ - P * j
                            for t in range(2):
                                mm = product(ps[:, 4 + j, 0:n], [v[:, t, P * j:P * (j + 1)] for v in (kh, kl)],
                                             [v[:, t, P * j:SEQ] for v in (qh, ql)], t == 0, t == 1)
                            mm.then_inc(scores_done, c.made(scores_done))
                        unit_v(X)
                        unit8(X)
                        pe.wait_ge(unit_taken, c.unit.value(-1))
                        pe.wait_ge(pt_ready, c.next(pt_ready, 4))
                        for i in range(ST):
                            if i >= 2:
                                pe.wait_ge(o_copied, c.next(o_copied))
                            for j in range(i + 1):
                                at = BY_KEY[j] + P * (i - j)
                                mm = product(ps[:, 6 + i % 2, :], [v[:, at:at + P] for v in (pth, ptl)],
                                             [v[:, 4 + j, :] for v in (hh, hl)], j == 0, j == i)
                            mm.then_inc(mixed_done, c.made(mixed_done))
                        unit8(X)
                        unit8(X)
                        pe.wait_ge(o_copied, c.next(o_copied, 2))
                        pe.wait_ge(p_ready, c.next(p_ready, 4))
                        for j in range(4):
                            for i in range(ST):
                                mm = nc.tensor.transpose(ps[:, 4 + j, P * i:P * (i + 1)],
                                                         o_sb[:, i, P * j:P * (j + 1)], ident[:, :])
                            mm.then_inc(turned, c.made(turned))
                        unit8(X)
                        unit4(H, 0, ready=hid_ready, fresh=True)
                        for _ in range(3):
                            unit4(H, 0)
                    head(0, True)
                    c.repeat(RET_HEADS - 1, head)
                    order = K4_ORDER
                if f in ("mlp0", "mlp1"):
                    def chunk(i, first=False):
                        if first:
                            first_units(order)
                        for _ in range(4 if first else 0, 8):
                            unit8(X)
                        unit_pair(H, ready=hid_ready)
                        for _ in range(6):
                            unit8(H)
                    chunk(0, True)
                    c.repeat(MLP_CHUNKS - 1, chunk)
                    order = NATURAL
                if f == "att":
                    banks[0] = 2

                    def qk_unit(n, between=None):
                        slot0 = (c.unit.n - n) // 2 % 2
                        unit8(X, slot=(slot0 + n % 2) % 2, half=n // 2, ahead=(1, 2, 0, 1)[n], between=between)

                    def unit4_narrow(n):
                        unit4(H, 0, fresh=True, bank0=0)

                    def scores(h, tiles):
                        if h % 2 == 0 and 0 in tiles:
                            pe.wait_ge(qk_ready, c.next(qk_ready, 2))
                        t, rows = h % 4 // 2, slice(64 * (h % 2), 64 * (h % 2) + 64)
                        for i in tiles:
                            bank, at = SCORES[i]
                            n = P * (i + 1)
                            if i == 0 and h:
                                pe.wait_ge(s_taken, ST * h)
                            if i == 1:
                                pe.wait_ge(s_taken, ST * h + 2)
                            mm = product(ps[:, bank, at:at + n], [v[rows, t, P * i:P * (i + 1)] for v in (qh, ql)],
                                         [v[rows, t, 0:n] for v in (kh, kl)], True, True)
                            if i != 0:
                                mm.then_inc(scores_done, c.made(scores_done))

                    def turn(h):
                        pe.wait_ge(p_ready, c.next(p_ready))
                        for bank, at, n in TURNED:
                            for j in range(ST):
                                if not at <= BY_KEY[j] < at + n:
                                    continue
                                for i in range(j, ST):
                                    src = BY_QUERY[i] + P * j
                                    o = BY_KEY[j] - at + P * (i - j)
                                    mm = nc.tensor.transpose(ps[:, bank, o:o + P], probs[:, h % 2, src:src + P], ident[:, :])
                            mm.then_inc(turned, c.made(turned))

                    def mix(h):
                        if h:
                            pe.wait_ge(hid_ready, c.next(hid_ready))
                        pe.wait_ge(pt_ready, c.next(pt_ready, len(TURNED)))
                        for j in range(ST):
                            t = h % 4 // 2
                            n = SEQ - P * j
                            mm = product(ps[:, 7, P * j:SEQ], [v[:, j, P * t:P * (t + 1)] for v in (avh, avl)],
                                         [v[:, BY_KEY[j]:BY_KEY[j] + n] for v in (pth, ptl)], j == 0, j == ST - 1)
                        mm.then_inc(mixed_done, c.made(mixed_done))

                    banks[0] = 4
                    unit_pair(X, order=order, ready=x_ready, fresh=True, across=True, between=stats)
                    qk_unit(2, between=spread)
                    qk_unit(3)
                    banks[0] = 2
                    unit_v(X)
                    pe.wait_ge(unit_taken, c.unit.n - 1)
                    scores(0, SCORES)
                    unit_v(X)
                    v_units = c.unit.n
                    scores(1, (0, 2, 3))
                    turn(0)
                    scores(1, (1,))
                    for h in range(1, ATT_HEADS):
                        s, last_group = h % 4, h >= ATT_HEADS - 4
                        if s == 0:
                            qk_unit(3)
                            mix(h - 1)
                            unit_v(X)
                            scores(h + 1, (0, 2, 3))
                            turn(h)
                            scores(h + 1, (1,))
                            unit_v(X)
                            v_units = c.unit.n
                            continue
                        if last_group:
                            unit4_narrow(s - 1)
                        else:
                            qk_unit(s - 1)
                        if h + 1 < ATT_HEADS:
                            scores(h + 1, (0, 2, 3))
                        if s == 1:
                            pe.wait_ge(unit_taken, v_units)
                        mix(h - 1)
                        if h + 1 < ATT_HEADS:
                            scores(h + 1, (1,))
                        turn(h)
                    unit4_narrow(3)
                    mix(ATT_HEADS - 1)
                    banks[0] = 4
                    pe.wait_ge(hid_ready, c.next(hid_ready, 1))
                    unit4(H, 4, fresh=True)
                    for _ in range(3):
                        unit4(H, 4)
                    order = K4_ORDER

            stats()
            spread()

        @block.scalar
        def _(act):
            c = Counts(act, sems)
            act.dma_start(prm[:, :], params).then_inc(p_landed, 16)
            for i in range(X_LOADS):
                n = KT // X_LOADS
                if i:
                    act.dma_start(x[:, n * i:n * (i + 1), :], x_tiles[:, n * i:n * (i + 1), :]).then_inc(x_landed[i], 16)
            act.dma_start(ident[:, :], ident_c).then_inc(c_landed, 16)
            act.dma_start(ext[:, 255:575], rel_bias).then_inc(ext_landed, 16)

            def convert(n=1):
                for _ in range(n):
                    place = c.of[w_hi]
                    halves = place.n
                    if place.turn is None and halves >= 2 * n_blocks:
                        return
                    slot, half = halves // 2 % 2, halves % 2
                    act.wait_ge(w_landed[slot], place.value(-(halves % 4)) * 4 + 16)
                    cut = (slice(None), slot, slice(None), slice(HALF * half, HALF * (half + 1)))
                    view = [t[:, :, :].rearrange("p s (k c) -> p s k c", c=256)[cut] for t in (wh, raw)]
                    nc.scalar.activation(view[0], view[1], ACT.Copy).then_inc(w_hi, c.made(w_hi))

            def after_unit():
                act.wait_ge(unit_done, c.next(unit_done))
                c.unit.n += 1
                convert()

            def make_root():
                act.wait_ge(to_curve, c.next(to_curve))
                nc.scalar.activation(root, ms, ACT.Sqrt).then_inc(curve_made, c.made(curve_made))

            def hi_of(dst, src):
                act.wait_ge(to_hi, c.next(to_hi))
                nc.scalar.activation(dst, src, ACT.Copy).then_inc(hi_made, c.made(hi_made))

            def prep(d, place, kind, name, row):
                act.wait_ge(x_added, c.next(x_added))
                if kind == "norm":
                    nc.scalar.activation(xh[:, d, :], x[:, d, :], ACT.Copy, scale=prow(name, row + d)).then_inc(hi_made, c.made(hi_made))
                nc.scalar.activation(squares[:, 2 * (place % 2), :], x[:, d, :], ACT.Square).then_inc(curve_made, c.made(curve_made))
                if kind == "norm":
                    return
                act.wait_ge(curve_made, c.now(curve_made))
                if kind == "final":
                    nc.scalar.activation(x[:, d, :], x[:, d, :], ACT.Copy, scale=prow(name, row + d)).then_inc(hi_made, c.made(hi_made))
                    return
                nc.scalar.activation(x[:, d, :], x[:, d, :], ACT.Copy, scale=prow("norm_final_g", d)).then_inc(act_step, c.made(act_step))
                act.wait_ge(act_step, c.now(act_step))
                nc.scalar.activation(xh[:, d, :], x[:, d, :], ACT.Copy, scale=prow(name, row + d)).then_inc(hi_made, c.made(hi_made))
                nc.scalar.activation(squares[:, 2 * (place % 2) + 1, :], x[:, d, :], ACT.Square).then_inc(curve_made, c.made(curve_made))

            def out_units8(prepare=None):
                for d in range(KT):
                    if prepare:
                        prep(d, d, *prepare)
                    after_unit()

            def out_units4(prepare=None):
                for n, d in enumerate(K4_ORDER):
                    if prepare:
                        prep(d, n, *prepare)
                    if n % 2:
                        after_unit()

            def taken():
                act.wait_ge(unit_taken, c.unit.value(1))

            def value_hi(dst, c0):
                act.wait_ge(unit_done, c.unit.value(1))
                u, half = c.unit.n, c.unit.n % 2
                for m in range(2):
                    s = 2 * half + m
                    last = nc.scalar.activation(dst[:, s, c0:c0 + 256], ps[:, u % banks[0], 256 * m:256 * (m + 1)],
                                                ACT.Copy, scale=rc[:, s:s + 1])
                last.then_inc(hi_made, c.made(hi_made))

            def load_bias(h):
                for p0, n in ((0, 448), (64, SEQ)):
                    act.dma_start(bias[p0:p0 + 64, h % 4, 0:n], bias_dram[h, p0:p0 + 64, 0:n]).then_inc(bias_landed[h % 4], 16)

            act.wait_ge(ones_set, 1)
            nc.scalar.activation(cols[:, 0:1], ones[:, 0:1], ACT.Copy).then_inc(act_step, c.made(act_step))
            banks = [4]
            convert(1)
            act.wait_ge(p_landed, 16)
            for d in range(KT):
                act.wait_ge(x_landed[d * X_LOADS // KT], 16)
                nc.scalar.activation(xh[:, d, :], x[:, d, :], ACT.Copy, scale=prow("norm_mix_g", d)).then_inc(
                    hi_made, c.made(hi_made))
                if d == 1:
                    convert(1)
                for k in range(4) if d == 3 else range(4, POOL_SQUARES[0]) if d == KT - 1 else ():
                    nc.scalar.activation(x_squares[:, k, :], x[:, k, :], ACT.Square).then_inc(curve_made, c.made(curve_made))
            convert(2)
            act.wait_ge(ext_built, 1)
            rows = ext[:, 0:SEQ]
            skewed = bass.AP(rows.tensor, rows.offset + P - 1, [rows.ap[0], [-1, P], [1, SEQ]])
            act.dma_start(bias_dram, skewed).then_inc(ext_stored, 16)
            for f in phases:
                nxt = next_prep(f)
                if f == "mix":
                    make_root()
                    for u in range(MIX_UNITS):
                        g = u - FIRST_TAP_UNIT + 2
                        if 0 <= g < TENSOR_TAPS:
                            for m in range(2):
                                last = nc.scalar.activation(tap_w[:, g % 4, m, :], ident[:, :], ACT.Copy,
                                                            scale=prow("conv_b_w", 4 * g + 2 + m))
                            last.then_inc(taps_made, c.made(taps_made))
                        after_unit()
                        if u in (3, 7):
                            for t in range(2):
                                act.wait_ge(unit_taken, c.unit.value(t - 1))
                                nc.scalar.activation(gbuf[:, t, :], gbuf[:, t, :], ACT.Sigmoid).then_inc(curve_made, c.made(curve_made))
                        if u >= 16:
                            hi_of(hh[:, u - 16, :], ybuf[:, u % 2, :])
                    after_unit()
                    for t in range(4):
                        act.wait_ge(to_curve, c.next(to_curve))
                        nc.scalar.activation(ln_squares[t], cacc[:, t, :], ACT.Square).then_inc(curve_made, c.made(curve_made))
                    after_unit()
                    make_root()
                    after_unit()
                    for t in range(4):
                        act.wait_ge(to_curve, c.next(to_curve))
                        nc.scalar.activation(cacc[:, t, :], cacc[:, t, :], ACT.Silu, scale=prow("ln_b_g", t),
                                                   bias=prow("ln_b_b", t)).then_inc(act_step, c.made(act_step))
                        act.wait_ge(*c.own())
                        nc.scalar.activation(hh[:, 4 + t, :], cacc[:, t, :], ACT.Copy).then_inc(hi_made, c.made(hi_made))
                    after_unit()
                    out_units4(nxt)
                if f == "ffn":
                    for dst, src in ((cos, cos_c), (sin, sin_c), (decay, decay_c)) if "ret" in phases else ():
                        act.dma_start(dst, src).then_inc(tab_landed, 16)
                    def chunk(i, tiles=8, prepare=None, first=False):
                        for b in range(tiles // 2):
                            ahead = first and b == 0
                            if ahead:
                                after_unit()
                                after_unit()
                            for t in range(2):
                                if not ahead:
                                    after_unit()
                                act.wait_ge(to_curve, c.next(to_curve))
                                nc.scalar.activation(gact[:, t, :], gconv[:, t, :], ACT.Silu).then_inc(curve_made, c.made(curve_made))
                            for t in range(2):
                                after_unit()
                                hi_of(hh[:, 2 * b + t, :], hval[:, t, :])
                        out_units8(prepare)
                    make_root()
                    chunk(0, first=True)
                    chunk(1)
                    chunk(2, 6, nxt)
                if f == "ret":
                    def head(h, prepare=None):
                        for dst in (qh, kh):
                            after_unit()
                            after_unit()
                            hi_of(dst[:, :, :], sg[:, 0:2, :])
                            if h == 0 and dst is qh:
                                make_root()

                        def v_unit(n):
                            value_hi(hh[:, 4:8, :], 256 * (n // 2))
                            act.wait_ge(unit_done, c.next(unit_done))
                            c.unit.n += 1
                            if n % 2:
                                convert(2)
                        for n in range(3):
                            v_unit(n)
                        for j in range(ST):
                            act.wait_ge(to_hi, c.next(to_hi))
                            cut = slice(BY_KEY[j], BY_KEY[j] + SEQ - P * j)
                            nc.scalar.activation(pth[:, cut], ptf[:, cut], ACT.Copy).then_inc(hi_made, c.made(hi_made))
                        v_unit(3)

                        def gate(j):
                            taken()
                            nc.scalar.activation(sg[:, j, :], sg[:, j, :], ACT.Silu).then_inc(curve_made, c.made(curve_made))
                            after_unit()
                        after_unit()
                        for i in range(ST):
                            act.wait_ge(mixed_done, c.next(mixed_done))
                            nc.scalar.activation(o_sb[:, i, :], ps[:, 6 + i % 2, :], ACT.Copy).then_inc(o_copied, c.made(o_copied))
                        act.wait_ge(unit_taken, c.unit.value(0))
                        nc.scalar.activation(sg[:, 0, :], sg[:, 0, :], ACT.Silu).then_inc(curve_made, c.made(curve_made))
                        make_root()
                        gate(1)
                        gate(2)
                        for j in range(3):
                            hi_of(hh[:, j, :], sg[:, j, :])
                        gate(3)
                        hi_of(hh[:, 3, :], sg[:, 3, :])
                        out_units4(prepare)
                    make_root()
                    head(0)
                    head(1)
                    head(2)
                    head(3, nxt)
                if f in ("mlp0", "mlp1"):
                    if f == "mlp0" and "att" in phases:
                        act.wait_ge(ext_stored, 16)
                        for h in range(4):
                            load_bias(h)
                    def chunk(i, prepare=None, first=False):
                        for u in range(8):
                            for _ in range((2, 0, 1, 1, 1, 1, 1, 1)[u] if first else 1):
                                after_unit()
                            hi_of(hh[:, u, :], hval[:, u % 2, :])
                        out_units8(prepare)
                    make_root()
                    chunk(0, first=True)
                    chunk(1)
                    chunk(2)
                    chunk(MLP_CHUNKS - 1, nxt)
                if f == "att":
                    banks[0] = 2
                    make_root()

                    def qk_done(n):
                        act.wait_ge(unit_done, c.next(unit_done))
                        c.unit.n += 1
                        convert((1, 0, 2, 1)[n])

                    def qk_hi(n, later=0):
                        act.wait_ge(unit_taken, c.unit.value(-later))
                        dst = (qh, kh)[n % 2]
                        nc.scalar.activation(dst[:, n // 2, :], hval[:, n % 2, :], ACT.Copy).then_inc(hi_made, c.made(hi_made))

                    def qk_unit(n):
                        qk_hi(n, -1)
                        qk_done(n)

                    def v_unit(n):
                        value_hi(avh, 0)
                        act.wait_ge(unit_done, c.next(unit_done))
                        c.unit.n += 1
                        if n:
                            convert(2)

                    def exps(h):
                        act.wait_ge(to_curve, c.next(to_curve))
                        for i in range(ST):
                            cut = slice(BY_QUERY[i], BY_QUERY[i] + P * (i + 1))
                            last = nc.scalar.activation(probs[:, h % 2, cut], probs[:, h % 2, cut], ACT.Exp,
                                                        bias=nmx[:, i:i + 1], accum_out=rs[:, i:i + 1])
                        last.then_inc(curve_made, c.made(curve_made))
                        if h + 4 < ATT_HEADS:
                            load_bias(h + 4)

                    def probs_hi():
                        for bank, at, n in TURNED:
                            act.wait_ge(turned, c.next(turned))
                            nc.scalar.activation(pth[:, at:at + n], ps[:, bank, 0:n], ACT.Copy).then_inc(hi_made, c.made(hi_made))

                    def mixed_hi(h):
                        rows = slice(64 * (h % 2), 64 * (h % 2) + 64)
                        act.wait_ge(mixed_done, c.next(mixed_done))
                        nc.scalar.activation(hh[rows, h // 2, :], ps[rows, 7, :], ACT.Copy).then_inc(hi_made, c.made(hi_made))

                    qk_done(0)
                    qk_done(1)
                    qk_hi(0, 1)
                    qk_hi(1)
                    for n in (2, 3):
                        qk_done(n)
                        qk_hi(n)
                    c.of[turned].n = turned_before_att
                    v_unit(0)
                    exps(0)
                    v_unit(1)
                    probs_hi()
                    exps(1)
                    for h in range(1, ATT_HEADS):
                        s, last_group = h % 4, h >= ATT_HEADS - 4
                        if s == 0:
                            qk_unit(3)
                            mixed_hi(h - 1)
                            v_unit(0)
                            probs_hi()
                            exps(h + 1)
                            v_unit(1)
                            continue
                        if last_group:
                            after_unit()
                        else:
                            qk_unit(s - 1)
                        mixed_hi(h - 1)
                        if h + 1 < ATT_HEADS:
                            exps(h + 1)
                        probs_hi()
                    after_unit()
                    mixed_hi(ATT_HEADS - 1)
                    banks[0] = 4
                    out_units4(nxt)
            make_root()

        @block.vector
        def _(dve):
            c = Counts(dve, sems)
            V = nc.vector
            banks = [4]

            def bank():
                return ps[:, c.unit.n % banks[0], :]

            def refine(signal=dve_step):
                dve.wait_ge(curve_made, c.next(curve_made))
                V.reciprocal(rc, root).then_inc(dve_step, c.made(dve_step))
                dve.wait_ge(dve_step, c.now(dve_step))
                V.tensor_tensor(t4, rc, rc, ALU.mult).then_inc(dve_step, c.made(dve_step))
                dve.wait_ge(dve_step, c.now(dve_step))
                V.tensor_tensor(t4, t4, ms, ALU.mult).then_inc(dve_step, c.made(dve_step))
                dve.wait_ge(dve_step, c.now(dve_step))
                V.tensor_scalar(t4, t4, -0.5, 1.5, ALU.mult, ALU.add).then_inc(dve_step, c.made(dve_step))
                dve.wait_ge(dve_step, c.now(dve_step))
                V.tensor_tensor(rc, rc, t4, ALU.mult).then_inc(signal, c.made(signal))
                dve.wait_ge(signal, c.now(signal))

            def mean_square(n, eps):
                V.tensor_scalar(ms, ps[:, 4, 0:ST], 1.0 / n, eps, ALU.mult, ALU.add).then_inc(to_curve, c.made(to_curve))

            def diagonals(col, spread=True):
                for i in range(ST):
                    V.tensor_scalar(diag[:, i, :], ident[:, :], col[:, i:i + 1], None, ALU.mult).then_inc(
                        dve_step if i < ST - 1 else stats_in, c.made(dve_step if i < ST - 1 else stats_in))
                if spread:
                    dve.wait_ge(stats_done, c.next(stats_done))

            def spread_factor():
                dve.wait_ge(stats_done, c.next(stats_done))
                mean_square(D, EPS)
                refine()
                diagonals(rc)

            def factor():
                spread_factor()
                V.tensor_copy(r_bc[:, :], ps[:, 5, :]).then_inc(dve_step, c.made(dve_step))
                dve.wait_ge(dve_step, c.now(dve_step))

            def input_lo(d, name, row):
                dve.wait_ge(hi_made, c.next(hi_made))
                V.scalar_tensor_tensor(xl[:, d, :], x[:, d, :], prow(name, row + d), xh[:, d, :].bitcast(F32),
                                       ALU.mult, ALU.subtract).then_inc(x_ready, c.made(x_ready))

            def start_sums(prepare, signal):
                if prepare[0] == "double":
                    V.memset(r_bc[:, :], 0.0).then_inc(dve_step, c.made(dve_step))
                V.memset(ssq[:, :], 0.0).then_inc(signal, c.made(signal))

            def next_input(d, place, prepare, signal, last):
                kind, name, row = prepare

                def add_squares(total, which, signal):
                    dve.wait_ge(curve_made, c.next(curve_made))
                    dve.wait_ge(*c.own())
                    V.tensor_tensor(total[:, :], total[:, :], squares[:, 2 * (place % 2) + which, :], ALU.add).then_inc(
                        signal, c.made(signal))

                if kind == "double":
                    add_squares(ssq, 0, signal)
                    input_lo(d, name, row)
                    add_squares(r_bc, 1, stats_in if last else dve_step)
                else:
                    add_squares(ssq, 0, stats_in if last else signal)
                    if kind == "norm":
                        input_lo(d, name, row)

            def finish_tile(order, n, prepare, signal):
                if n == 0:
                    start_sums(prepare, signal)
                else:
                    next_input(order[n - 1], n - 1, prepare, signal, False)
                if n == KT - 1:
                    next_input(order[n], n, prepare, dve_step, True)

            def out_units8(prepare=None):
                for d in range(KT):
                    dve.wait_ge(unit_done, c.next(unit_done))
                    signal = x_added if prepare else unit_taken
                    V.tensor_tensor(x[:, d, :], x[:, d, :], bank(), ALU.add).then_inc(signal, c.made(signal))
                    if prepare:
                        finish_tile(NATURAL, d, prepare, unit_taken)
                    c.unit.n += 1

            def out_units4(prepare=None, between=None):
                for n, d in enumerate(K4_ORDER):
                    half, m = n // 2 % 2, n % 2
                    if m == 0:
                        dve.wait_ge(unit_done, c.next(unit_done))
                    ends = unit_taken if m else dve_step
                    signal = x_added if prepare else ends
                    V.tensor_tensor(x[:, d, :], x[:, d, :], ps[:, 2 * half + m, :], ALU.add).then_inc(signal, c.made(signal))
                    if prepare:
                        finish_tile(K4_ORDER, n, prepare, ends)
                    if m:
                        c.unit.n += 1
                        if between:
                            between(n // 2)

            def scaled(dst, name=unit_taken, scale=None):
                dve.wait_ge(unit_done, c.next(unit_done))
                if scale is None:
                    i = V.tensor_tensor(dst, bank(), r_bc[:, :], ALU.mult)
                else:
                    i = V.scalar_tensor_tensor(dst, bank(), scale, r_bc[:, :], ALU.mult, ALU.mult)
                i.then_inc(name, c.made(name))
                c.unit.n += 1

            def hid_lo(k, src):
                dve.wait_ge(hi_made, c.next(hi_made))
                V.tensor_tensor(hl[:, k, :], src, hh[:, k, :].bitcast(F32), ALU.subtract).then_inc(hid_ready, c.made(hid_ready))

            dve.wait_ge(p_landed, 16)
            for first in (0, 4):
                for d in range(first, first + 4):
                    dve.wait_ge(x_landed[d * X_LOADS // KT], 16)
                    input_lo(d, "norm_mix_g", 0)
                for d in range(first, first + 4):
                    source = pool_squared if d in POOL_SQUARES else curve_made
                    dve.wait_ge(source, c.next(source))
                    if d == 0:
                        continue
                    dve.wait_ge(*c.own())
                    so_far = x_squares[:, 0, :] if d == 1 else ssq[:, :]
                    signal = stats_in if d == KT - 1 else dve_step
                    V.tensor_tensor(ssq[:, :], so_far, x_squares[:, d, :], ALU.add).then_inc(signal, c.made(signal))
            dve.wait_ge(*c.own())
            dve.wait_ge(ext_landed, 16)
            V.tensor_copy(ext[:, 0:255], ext[:, 255:256].to_broadcast([ATT_HEADS, 255])).then_inc(dve_step, c.made(dve_step))
            V.memset(ext[:, 575:640], 0.0).then_inc(ext_built, c.made(ext_built))
            dve.wait_ge(c_landed, 16)
            V.memset(upad[:, :, 0:PADC], 0.0).then_inc(dve_step, c.made(dve_step))
            V.memset(upad[:, :, PADC + SEQ:UPW], 0.0).then_inc(dve_step, c.made(dve_step))
            V.memset(apad[:, :, 0:1], 0.0).then_inc(dve_step, c.made(dve_step))
            V.memset(apad[:, :, SEQ + 1:SEQ + 2], 0.0).then_inc(dve_step, c.made(dve_step))

            for f in phases:
                nxt = next_prep(f)
                if f == "mix":
                    factor()

                    conv_at = list(FIRST_TAP)

                    def conv(pair, taps):
                        for _ in range(taps):
                            for t in (2 * pair, 2 * pair + 1):
                                k = conv_at[t]
                                if k == TAPS:
                                    continue
                                conv_at[t] += 1
                                first, last = k == FIRST_TAP[t], k == TAPS - 1
                                dve.wait_ge(dve_step, c.of[dve_step].n - (0 if first or last else 1))
                                src, w = upad[:, t, k:k + SEQ], prow("conv_b_w", 4 * k + t)
                                signal = conv_done if last and t < 2 else dve_step
                                if first:
                                    i = V.tensor_scalar(cacc[:, t, :], src, w, prow("conv_b_b", t), ALU.mult, ALU.add)
                                else:
                                    i = V.scalar_tensor_tensor(cacc[:, t, :], src, w, cacc[:, t, :], ALU.mult, ALU.add)
                                i.then_inc(signal, c.made(signal))

                    def conv_step():
                        if conv_at[1] < TAPS:
                            conv(0, 4)
                        elif c.unit.n >= 8:
                            conv(1, 4)

                    for j in range(2):
                        for t in range(2):
                            scaled(upad[:, 2 * j + t, PADC:PADC + SEQ])
                            if j:
                                conv_step()
                        for t in range(2):
                            scaled(gbuf[:, t, :])
                        for t in range(2):
                            dve.wait_ge(curve_made, c.next(curve_made))
                            u = upad[:, 2 * j + t, PADC:PADC + SEQ]
                            signal = u_ready if (j, t) == (1, 1) else dve_step
                            V.tensor_tensor(u, u, gbuf[:, t, :], ALU.mult).then_inc(signal, c.made(signal))
                            dve.wait_ge(signal, c.now(signal))
                        if j:
                            conv_step()
                    for t in range(4):
                        scaled(apad[:, t, 1:1 + SEQ])
                        conv_step()
                    for t in range(4):
                        scaled(gbuf[:, t % 2, :])
                        dve.wait_ge(*c.own())
                        a = apad[:, t, 1:1 + SEQ]
                        V.tensor_tensor(a, a, gbuf[:, t % 2, :], ALU.mult).then_inc(dve_step, c.made(dve_step))
                        dve.wait_ge(dve_step, c.now(dve_step))
                        conv_step()
                    dve.wait_ge(ext_stored, 16)
                    for t in range(4):
                        y = ybuf[:, t % 2, :]
                        if t >= 1:
                            hid_lo(t - 1, ybuf[:, (t - 1) % 2, :])
                        scaled(gbuf[:, t % 2, :])
                        V.tensor_scalar(y, apad[:, t, 0:SEQ], prow("conv_a_w", t), None, ALU.mult).then_inc(dve_step, c.made(dve_step))
                        dve.wait_ge(dve_step, c.now(dve_step))
                        for k in (1, 2):
                            V.scalar_tensor_tensor(y, apad[:, t, k:k + SEQ], prow("conv_a_w", 4 * k + t), y,
                                                           ALU.mult, ALU.add).then_inc(dve_step, c.made(dve_step))
                            dve.wait_ge(dve_step, c.now(dve_step))
                        V.tensor_tensor(y, y, gbuf[:, t % 2, :], ALU.mult).then_inc(to_hi, c.made(to_hi))
                        dve.wait_ge(to_hi, c.now(to_hi))
                        conv_step()
                    hid_lo(3, ybuf[:, 1, :])
                    while conv_at[3] < TAPS:
                        conv_step()
                    dve.wait_ge(*c.own())
                    dve.wait_ge(taps_done, c.next(taps_done))
                    for t in (2, 3):
                        V.tensor_tensor(cacc[:, t, :], cacc[:, t, :], ps[:, 4 + t, :], ALU.add).then_inc(conv_done, c.made(conv_done))

                    tiles = [cacc[:, t, :] for t in range(4)]

                    def layer_norm(n):
                        if n == 0:
                            dve.wait_ge(stats_done, c.next(stats_done))
                            dve.wait_ge(*c.own())
                            for t in tiles:
                                V.scalar_tensor_tensor(t, ps[:, 5, :], -1.0 / D_A, t, ALU.mult, ALU.add).then_inc(
                                    to_curve, c.made(to_curve))
                            dve.wait_ge(curve_made, c.next(curve_made, 2))
                            V.tensor_tensor(ssq[:, :], ln_squares[0], ln_squares[1], ALU.add).then_inc(dve_step, c.made(dve_step))
                            for t in (2, 3):
                                dve.wait_ge(dve_step, c.now(dve_step))
                                dve.wait_ge(curve_made, c.next(curve_made))
                                signal = stats_in if t == 3 else dve_step
                                V.tensor_tensor(ssq[:, :], ssq[:, :], ln_squares[t], ALU.add).then_inc(signal, c.made(signal))
                        if n == 1:
                            dve.wait_ge(stats_done, c.next(stats_done))
                            mean_square(D_A, LN_EPS)
                            refine()
                            diagonals(rc)
                        if n == 2:
                            for t in tiles:
                                V.tensor_tensor(t, t, ps[:, 5, :], ALU.mult).then_inc(to_curve, c.made(to_curve))
                            for t in range(4):
                                hid_lo(4 + t, tiles[t])

                    out_units4(between=layer_norm)
                    out_units4(nxt)
                if f == "ffn":
                    V.memset(gpad[:, :, 0:1], 0.0).then_inc(dve_step, c.made(dve_step))
                    V.memset(gpad[:, :, SEQ + 1:SEQ + 2], 0.0).then_inc(dve_step, c.made(dve_step))

                    def chunk(i, tiles=8, prepare=None):
                        for b in range(tiles // 2):
                            for t in range(2):
                                w = [prow("conv_ffn_w", (FF // P) * k + 8 * i + 2 * b + t) for k in range(3)]
                                scaled(gpad[:, t, 1:1 + SEQ])
                                dve.wait_ge(*c.own())
                                g = gconv[:, t, :]
                                V.tensor_scalar(g, gpad[:, t, 0:SEQ], w[0], None, ALU.mult).then_inc(dve_step, c.made(dve_step))
                                dve.wait_ge(dve_step, c.now(dve_step))
                                V.scalar_tensor_tensor(g, gpad[:, t, 1:1 + SEQ], w[1], g, ALU.mult, ALU.add).then_inc(dve_step, c.made(dve_step))
                                dve.wait_ge(dve_step, c.now(dve_step))
                                V.scalar_tensor_tensor(g, gpad[:, t, 2:2 + SEQ], w[2], g, ALU.mult, ALU.add).then_inc(to_curve, c.made(to_curve))
                                if b and not t:
                                    hid_lo(2 * b - 1, hval[:, 1, :])
                            for t in range(2):
                                scaled(hval[:, t, :])
                                dve.wait_ge(*c.own())
                                dve.wait_ge(curve_made, c.next(curve_made))
                                V.tensor_tensor(hval[:, t, :], hval[:, t, :], gact[:, t, :], ALU.mult).then_inc(to_hi, c.made(to_hi))
                                if t:
                                    hid_lo(2 * b, hval[:, 0, :])
                        hid_lo(tiles - 1, hval[:, 1, :])
                        out_units8(prepare)
                    factor()
                    chunk(0)
                    chunk(1)
                    chunk(2, 6, nxt)
                if f == "ret":
                    dve.wait_ge(stats_done, c.next(stats_done))
                    V.tensor_scalar(r1c, ps[:, 4, 0:ST], 1.0 / D, EPS, ALU.mult, ALU.add).then_inc(dve_step, c.made(dve_step))
                    V.tensor_scalar(ms2, ps[:, 4, ST:2 * ST], 1.0 / D, None, ALU.mult).then_inc(dve_step, c.made(dve_step))
                    dve.wait_ge(dve_step, c.now(dve_step))
                    V.scalar_tensor_tensor(ms, r1c, EPS, ms2, ALU.mult, ALU.add).then_inc(to_curve, c.made(to_curve))
                    dve.wait_ge(to_curve, c.now(to_curve))
                    refine()
                    diagonals(rc)
                    V.tensor_copy(r_bc[:, :], ps[:, 5, :]).then_inc(dve_step, c.made(dve_step))
                    dve.wait_ge(dve_step, c.now(dve_step))
                    dve.wait_ge(tab_landed, 48)
                    for t in (cos, sin):
                        V.tensor_tensor(t, t, r_bc[:, :], ALU.mult).then_inc(dve_step, c.made(dve_step))
                    dve.wait_ge(*c.own())

                    def rope(hi, lo, take_r1=False):
                        dve.wait_ge(unit_done, c.next(unit_done))
                        dve.wait_ge(unit_done, c.next(unit_done))
                        a, b = ps[:, c.unit.n % 4, :], ps[:, (c.unit.n + 1) % 4, :]
                        V.tensor_tensor(sg[:, 0, :], a, cos, ALU.mult).then_inc(dve_step, c.made(dve_step))
                        V.tensor_tensor(sg[:, 1, :], a, sin, ALU.mult).then_inc(dve_step, c.made(dve_step))
                        V.tensor_tensor(sg[:, 2, :], b, sin, ALU.mult).then_inc(dve_step, c.made(dve_step))
                        V.tensor_tensor(sg[:, 3, :], b, cos, ALU.mult).then_inc(unit_taken, c.made(unit_taken, 2))
                        dve.wait_ge(unit_taken, c.now(unit_taken))
                        V.tensor_tensor(sg[:, 0, :], sg[:, 0, :], sg[:, 2, :], ALU.subtract).then_inc(dve_step, c.made(dve_step))
                        V.tensor_tensor(sg[:, 1, :], sg[:, 1, :], sg[:, 3, :], ALU.add).then_inc(to_hi, c.made(to_hi))
                        c.unit.n += 2
                        if take_r1:
                            dve.wait_ge(stats_done, c.next(stats_done))
                            V.tensor_copy(ssq[:, :], ps[:, 5, :]).then_inc(dve_step, c.made(dve_step))
                        dve.wait_ge(hi_made, c.next(hi_made))
                        dve.wait_ge(*c.own())
                        V.tensor_tensor(lo[:, :, :], sg[:, 0:2, :], hi[:, :, :].bitcast(F32), ALU.subtract).then_inc(qk_ready, c.made(qk_ready))
                        dve.wait_ge(*c.own())

                    def score_lo(j):
                        cut = slice(BY_KEY[j], BY_KEY[j] + SEQ - P * j)
                        dve.wait_ge(hi_made, c.next(hi_made))
                        V.tensor_tensor(ptl[:, cut], ptf[:, cut], pth[:, cut].bitcast(F32), ALU.subtract).then_inc(
                            pt_ready, c.made(pt_ready))

                    def head(h, prepare=None, first=False):
                        rope(qh, ql)
                        if first:
                            V.tensor_copy(ms, r1c).then_inc(to_curve, c.made(to_curve))
                            refine_root()
                            diagonals(rc2, spread=False)
                        rope(kh, kl, take_r1=first)

                        def v_unit(n):
                            value_lo(hh[:, 4:8, :], hl[:, 4:8, :], 256 * (n // 2))
                        for n in range(3):
                            v_unit(n)
                        for j in range(ST):
                            dve.wait_ge(scores_done, c.next(scores_done))
                            n = SEQ - P * j
                            cut = slice(BY_KEY[j], BY_KEY[j] + n)
                            dec = decay[:, h, 0:n] if isinstance(h, int) else \
                                decay[:, bass.ds(h, 1), 0:n].rearrange("p a b -> p (a b)")
                            V.tensor_tensor(ptf[:, cut], ps[:, 4 + j, 0:n], dec, ALU.mult).then_inc(to_hi, c.made(to_hi))
                            if j:
                                score_lo(j - 1)
                        score_lo(ST - 1)
                        v_unit(3)
                        scaled(sg[:, 0, :])
                        c.next(curve_made)
                        for i in range(ST):
                            dve.wait_ge(o_copied, c.next(o_copied))
                            V.bn_stats(bn, o_sb[:, i, :]).then_inc(dve_step, c.made(dve_step))
                            dve.wait_ge(dve_step, c.now(dve_step))
                            V.bn_aggr(mv[:, i, :], bn).then_inc(dve_step, c.made(dve_step))
                            dve.wait_ge(dve_step, c.now(dve_step))
                        V.tensor_scalar(ms, mv[:, :, 1], EPS, None, ALU.add).then_inc(to_curve, c.made(to_curve))
                        refine_root()
                        for i in range(ST):
                            V.tensor_scalar(o_sb[:, i, :], o_sb[:, i, :], mv[:, i, 0:1], rc2[:, i:i + 1],
                                                 ALU.subtract, ALU.mult).then_inc(p_ready, c.made(p_ready))
                        scaled(sg[:, 1, :])
                        scaled(sg[:, 2, :])

                        def gated(j):
                            dve.wait_ge(turned, c.next(turned))
                            if j:
                                dve.wait_ge(curve_made, c.next(curve_made))
                            g = prow("ret_gn_g_2", 4 * h + j)
                            V.scalar_tensor_tensor(sg[:, j, :], ps[:, 4 + j, :], g, sg[:, j, :], ALU.mult, ALU.mult).then_inc(to_hi, c.made(to_hi))

                        for j in range(3):
                            gated(j)
                            if j:
                                hid_lo(j - 1, sg[:, j - 1, :])
                        hid_lo(2, sg[:, 2, :])
                        scaled(sg[:, 3, :])
                        gated(3)
                        hid_lo(3, sg[:, 3, :])
                        if first:
                            for d in range(KT):
                                V.tensor_tensor(x[:, d, :], x[:, d, :], ssq[:, :], ALU.mult).then_inc(dve_step, c.made(dve_step))
                            dve.wait_ge(dve_step, c.now(dve_step))
                        out_units4(prepare)

                    rc2 = t4

                    def refine_root():
                        dve.wait_ge(curve_made, c.next(curve_made))
                        V.reciprocal(rc2, root).then_inc(dve_step, c.made(dve_step))
                        dve.wait_ge(dve_step, c.now(dve_step))
                        V.tensor_tensor(ms2, rc2, rc2, ALU.mult).then_inc(dve_step, c.made(dve_step))
                        dve.wait_ge(dve_step, c.now(dve_step))
                        V.tensor_tensor(ms2, ms2, ms, ALU.mult).then_inc(dve_step, c.made(dve_step))
                        dve.wait_ge(dve_step, c.now(dve_step))
                        V.tensor_scalar(ms2, ms2, -0.5, 1.5, ALU.mult, ALU.add).then_inc(dve_step, c.made(dve_step))
                        dve.wait_ge(dve_step, c.now(dve_step))
                        V.tensor_tensor(rc2, rc2, ms2, ALU.mult).then_inc(dve_step, c.made(dve_step))
                        dve.wait_ge(dve_step, c.now(dve_step))

                    def value_lo(hi, lo, c0):
                        dve.wait_ge(unit_done, c.next(unit_done))
                        dve.wait_ge(hi_made, c.next(hi_made))
                        half = c.unit.n % 2
                        for m in range(2):
                            s = 2 * half + m
                            signal = unit_taken if m else dve_step
                            V.scalar_tensor_tensor(lo[:, s, c0:c0 + 256], bank()[:, 256 * m:256 * (m + 1)], rc[:, s:s + 1],
                                                        hi[:, s, c0:c0 + 256].bitcast(F32), ALU.mult, ALU.subtract).then_inc(signal, c.made(signal))
                        c.unit.n += 1

                    head(0, first=True)
                    head(1)
                    head(2)
                    head(3, nxt)
                if f in ("mlp0", "mlp1"):
                    if f == "mlp0" and "att" in phases:
                        V.memset(bias[0:64, :, 448:512], MASKED).then_inc(dve_step, c.made(dve_step))
                    def chunk(i, prepare=None):
                        for u in range(8):
                            dve.wait_ge(unit_done, c.next(unit_done))
                            h = hval[:, u % 2, :]
                            dve.wait_ge(*c.own())
                            V.scalar_tensor_tensor(h, bank(), 0.0, r_bc[:, :], ALU.max, ALU.mult).then_inc(unit_taken, c.made(unit_taken))
                            dve.wait_ge(unit_taken, c.now(unit_taken))
                            c.unit.n += 1
                            V.tensor_tensor(h, h, h, ALU.mult).then_inc(to_hi, c.made(to_hi))
                            if u:
                                hid_lo(u - 1, hval[:, (u - 1) % 2, :])
                        hid_lo(KT - 1, hval[:, 1, :])
                        out_units8(prepare)
                    factor()
                    c.repeat(MLP_CHUNKS - 1, chunk)
                    chunk(MLP_CHUNKS - 1, nxt)
                if f == "att":
                    banks[0] = 2
                    factor()

                    def value_lo():
                        dve.wait_ge(unit_done, c.next(unit_done))
                        dve.wait_ge(hi_made, c.next(hi_made))
                        half = c.unit.n % 2
                        for m in range(2):
                            s = 2 * half + m
                            signal = unit_taken if m else dve_step
                            V.scalar_tensor_tensor(avl[:, s, :], bank()[:, 256 * m:256 * (m + 1)], rc[:, s:s + 1],
                                                        avh[:, s, :].bitcast(F32), ALU.mult, ALU.subtract).then_inc(signal, c.made(signal))
                        c.unit.n += 1

                    def qk_unit(n):
                        hi, lo = ((qh, ql), (kh, kl))[n % 2]
                        scaled(hval[:, n % 2, :], scale=0.125 if n % 2 == 0 else 1.0)
                        dve.wait_ge(hi_made, c.next(hi_made))
                        dve.wait_ge(*c.own())
                        V.tensor_tensor(lo[:, n // 2, :], hval[:, n % 2, :], hi[:, n // 2, :].bitcast(F32), ALU.subtract).then_inc(qk_ready, c.made(qk_ready))

                    def maxima(h, tiles=SCORES):
                        dve.wait_ge(bias_landed[h % 4], 32 * (h // 4 + 1))
                        for i in tiles:
                            bk, at = SCORES[i]
                            n = P * (i + 1)
                            if i != 2:
                                dve.wait_ge(scores_done, c.next(scores_done))
                            V.tensor_tensor_reduce(probs[:, h % 2, BY_QUERY[i]:BY_QUERY[i] + n], ps[:, bk, at:at + n],
                                                        bias[:, h % 4, SEQ - n:SEQ], 1.0, MASKED, ALU.add, ALU.max,
                                                        mx[:, i:i + 1]).then_inc(s_taken, c.made(s_taken))
                        if 1 not in tiles:
                            return
                        dve.wait_ge(*c.own())
                        V.tensor_scalar(nmx, mx, -1.0, None, ALU.mult).then_inc(to_curve, c.made(to_curve))

                    def normalise(h):
                        dve.wait_ge(curve_made, c.next(curve_made))
                        V.reciprocal(rinv, rs).then_inc(dve_step, c.made(dve_step))
                        dve.wait_ge(dve_step, c.now(dve_step))
                        for i in range(ST):
                            cut = slice(BY_QUERY[i], BY_QUERY[i] + P * (i + 1))
                            signal = p_ready if i == ST - 1 else dve_step
                            V.tensor_scalar(probs[:, h % 2, cut], probs[:, h % 2, cut], rinv[:, i:i + 1], None, ALU.mult).then_inc(signal, c.made(signal))

                    def probs_lo():
                        for bk, at, n in TURNED:
                            dve.wait_ge(hi_made, c.next(hi_made))
                            cut = slice(at, at + n)
                            V.tensor_tensor(ptl[:, cut], ps[:, bk, 0:n], pth[:, cut].bitcast(F32), ALU.subtract).then_inc(pt_ready, c.made(pt_ready))

                    def mixed_lo(h):
                        rows = slice(64 * (h % 2), 64 * (h % 2) + 64)
                        dve.wait_ge(hi_made, c.next(hi_made))
                        V.tensor_tensor(hl[rows, h // 2, :], ps[rows, 7, :], hh[rows, h // 2, :].bitcast(F32),
                                             ALU.subtract).then_inc(hid_ready, c.made(hid_ready))

                    def out_narrow(n):
                        dve.wait_ge(unit_done, c.next(unit_done))
                        for m in range(2):
                            d = K4_ORDER[2 * n + m]
                            signal = unit_taken if m else dve_step
                            V.tensor_tensor(x[:, d, :], x[:, d, :], ps[:, m, :], ALU.add).then_inc(signal, c.made(signal))
                        c.unit.n += 1

                    banks[0] = 4
                    for n in range(4):
                        qk_unit(n)
                    banks[0] = 2
                    value_lo()
                    maxima(0)
                    normalise(0)
                    value_lo()
                    maxima(1)
                    probs_lo()
                    normalise(1)
                    for h in range(1, ATT_HEADS):
                        s, last_group = h % 4, h >= ATT_HEADS - 4
                        if s == 0:
                            qk_unit(3)
                            mixed_lo(h - 1)
                            value_lo()
                            maxima(h + 1)
                            probs_lo()
                            normalise(h + 1)
                            value_lo()
                            continue
                        if last_group:
                            out_narrow(s - 1)
                        else:
                            qk_unit(s - 1)
                        if h + 1 < ATT_HEADS:
                            maxima(h + 1, (0, 2, 3))
                        mixed_lo(h - 1)
                        if h + 1 < ATT_HEADS:
                            maxima(h + 1, (1,))
                        probs_lo()
                        if h + 1 < ATT_HEADS:
                            normalise(h + 1)
                    out_narrow(3)
                    mixed_lo(ATT_HEADS - 1)
                    banks[0] = 4
                    out_units4(nxt)
            dve.wait_ge(hi_made, c.next(hi_made, KT))
            spread_factor()
            for n in range(KT):
                V.tensor_tensor(x[:, n, :], x[:, n, :], ps[:, 5, :], ALU.mult).then_inc(out_ready, 1)


PHASES = ["mix", "ffn", "ret", "mlp0", "att", "mlp1"]
WEIGHTS = ["w_in", "w_out", "w_gate", "w_up", "w_down", "ret_w_in_2", "ret_w_out_2", "att_w_in_2",
           "att_rel_bias_2", "att_w_out_2", "mlp_w1_2", "mlp_w2_2"]


def constants():
    half = D // RET_HEADS // 2
    f = np.float32
    inv = np.exp(-np.log(f(10000.0)) * np.arange(half, dtype=f) / f(half)).astype(f)
    angle = (inv[:, None] * np.arange(SEQ, dtype=f)[None, :]).astype(f).astype(np.float64)
    log_gamma = np.log1p(-np.exp2(-5.0 - np.arange(RET_HEADS)))
    key, query = np.arange(P)[:, None], np.arange(SEQ)[None, :]
    decay = np.exp(log_gamma[:, None, None] * np.abs(query - key)) * (query // 64 >= key // 64)
    decay = decay * (D // RET_HEADS) ** -0.5
    return {"ident": np.eye(P, dtype=f), "cos": np.cos(angle).astype(f), "sin": np.sin(angle).astype(f),
            "decay": np.ascontiguousarray(decay.transpose(1, 0, 2)).astype(f)}


def program(nc, a, phases=PHASES):
    consts = [a["const_ident"], a["const_cos"], a["const_sin"], a["const_decay"]]
    build(nc, phases, a["x"], a["w_in"][0], a["w_out"][0], a["w_gate"][0], a["w_up"][0], a["w_down"][0],
          a["ret_w_in_2"][0], a["ret_w_out_2"][0], a["att_w_in_2"][0], a["att_w_out_2"][0],
          [a["mlp_w1_2"][m] for m in range(2)], [a["mlp_w2_2"][m] for m in range(2)], a["att_rel_bias_2"][0],
          a["params"], consts, a["out"])


def laid_out(inputs):
    side_by_side = [np.asarray(inputs[name]).reshape(-1, P).T for name in ROWS]
    given = {name: np.ascontiguousarray(inputs[name]) for name in WEIGHTS}
    given["x"] = np.ascontiguousarray(np.asarray(inputs["x"])[0].T)
    given["params"] = np.ascontiguousarray(np.concatenate(side_by_side, axis=1))
    given.update({f"const_{name}": v for name, v in constants().items()})
    return given


def kernel(**inputs):
    import concourse.bacc as _bacc
    from concourse.bass_utils import run_bass_kernel_spmd as _run

    nc = _bacc.Bacc("TRN2", target_bir_lowering=False, num_devices=1)
    arrays, tensors = {}, {}
    for name, v in laid_out(inputs).items():
        arrays[f"in_{name}_dram"] = v
        tensors[name] = nc.dram_tensor(f"in_{name}_dram", v.shape, mybir.dt.from_np(v.dtype), kind="ExternalInput").ap()
    tensors["out"] = nc.dram_tensor("out_0_dram", (D, SEQ), F32, kind="ExternalOutput").ap()
    program(nc, tensors)
    r = _run(nc, [arrays], core_ids=[0])
    return np.ascontiguousarray(r.results[0]["out_0_dram"].T).reshape(1, SEQ, D)
```
